# Optimizing a Trainium2 kernel written in Bass

```python
import jax, jax.numpy as jnp
from jax import lax
import numpy as np

D_MODEL = 1024
BATCH = 1
SEQ = 256
DEPTH = 2
DEC_BATCH = 8
DEC_SEQ = 1
PAST_LEN = 256
PAGE_SIZE = 128

D_MIX = D_MODEL
HEAD_DIM = 64
GROUP_W = D_MIX // 4
C_A = GROUP_W
CONV_A_W = 31
H_B = GROUP_W // HEAD_DIM
DV_B = HEAD_DIM
DK_B = HEAD_DIM // 2
GLA_RANK = 16
GLA_TAU = 16.0
GLA_CHUNK = 64
C_C = GROUP_W
CONV_C_W = 3
H_D = GROUP_W // HEAD_DIM
DH_D = HEAD_DIM
Q_BLOCK = 128
FORGET_BIAS_INIT = 3.0
D_FF = ((8 * D_MODEL // 3 + 127) // 128) * 128
EPS = 1e-6
NEG_INF = -1e30

OFF_A = 0
N_A = 2 * C_A
OFF_B = OFF_A + N_A
N_B = 2 * H_B * DK_B + 2 * H_B * DV_B + GLA_RANK
OFF_C = OFF_B + N_B
N_C = 3 * C_C
OFF_D = OFF_C + N_C
N_D = 3 * H_D * DH_D + H_D
N_IN = OFF_D + N_D

kernel_name = 'hymba_style_conformer_gla_shortconv_fox_decoder_step'

F32 = jnp.float32

def rms_norm(x, g):
    xf = x.astype(F32)
    y = xf * lax.rsqrt(jnp.mean(xf * xf, axis=-1, keepdims=True) + EPS)
    return (y * g.astype(F32)).astype(x.dtype)

def layer_norm(x, g, b):
    xf = x.astype(F32)
    mu = jnp.mean(xf, axis=-1, keepdims=True)
    var = jnp.mean(jnp.square(xf - mu), axis=-1, keepdims=True)
    y = (xf - mu) * lax.rsqrt(var + EPS) * g.astype(F32) + b.astype(F32)
    return y.astype(x.dtype)

def swiglu(x, w_gate, w_up, w_down):
    return (jax.nn.silu(x @ w_gate) * (x @ w_up)) @ w_down

def causal_depthwise(xpad, w):
    c = xpad.shape[-1]
    return lax.conv_general_dilated(xpad, w.astype(xpad.dtype)[:, None, :], window_strides=(1,),
                                    padding='VALID', dimension_numbers=('NWC', 'WIO', 'NWC'),
                                    feature_group_count=c)

def conformer_conv(pa, buf, conv_w, conv_b, ln_g, ln_b):
    val, gate = jnp.split(pa, 2, axis=-1)
    a = val * jax.nn.sigmoid(gate)
    xpad = jnp.concatenate([buf.astype(a.dtype), a], axis=1)
    y = causal_depthwise(xpad, conv_w) + conv_b.astype(a.dtype)
    y = jax.nn.silu(layer_norm(y, ln_g, ln_b))
    return y, xpad[:, -(CONV_A_W - 1):]

def gla_chunked(q, k, v, log_a, s0, chunk):
    bsz, length, nh, dk = q.shape
    n = length // chunk

    def to_chunks(t):
        return t.reshape(bsz, n, chunk, *t.shape[2:]).swapaxes(0, 1)

    mask = jnp.tril(jnp.ones((chunk, chunk), bool))[None, :, :, None, None]

    def step(s, inp):
        qc, kc, vc, ac = inp
        b = jnp.cumsum(ac, axis=1)
        o_inter = jnp.einsum('bthk,bhkv->bthv', qc * jnp.exp(b), s)
        diff = b[:, :, None] - b[:, None, :]
        decay = jnp.exp(jnp.where(mask, diff, -jnp.inf))
        scores = jnp.einsum('bthk,bshk,btshk->bhts', qc, kc, decay)
        o_intra = jnp.einsum('bhts,bshv->bthv', scores, vc)
        b_last = b[:, -1]
        k_dec = kc * jnp.exp(b_last[:, None] - b)
        s_new = jnp.exp(b_last)[..., None] * s + jnp.einsum('bshk,bshv->bhkv', k_dec, vc)
        return s_new, o_inter + o_intra

    s_fin, o = lax.scan(step, s0, (to_chunks(q), to_chunks(k), to_chunks(v), to_chunks(log_a)))
    return o.swapaxes(0, 1).reshape(bsz, length, nh, v.shape[-1]), s_fin

def gla_mixer(pb, state, w_a2, b_a, norm_g):
    bsz, length, _ = pb.shape
    kd, vd = H_B * DK_B, H_B * DV_B
    q, k, v, g, a_lr = jnp.split(pb, [kd, 2 * kd, 2 * kd + vd, 2 * kd + 2 * vd], axis=-1)
    log_a = jax.nn.log_sigmoid((a_lr @ w_a2 + b_a).astype(F32)) / GLA_TAU
    q = q.astype(F32).reshape(bsz, length, H_B, DK_B) * (DK_B ** -0.5)
    k = k.astype(F32).reshape(bsz, length, H_B, DK_B)
    v = v.astype(F32).reshape(bsz, length, H_B, DV_B)
    log_a = log_a.reshape(bsz, length, H_B, DK_B)
    chunk = GLA_CHUNK if length % GLA_CHUNK == 0 else length
    o, s_new = gla_chunked(q, k, v, log_a, state.astype(F32), chunk)
    o = o * lax.rsqrt(jnp.mean(o * o, axis=-1, keepdims=True) + EPS)
    o = o.reshape(bsz, length, vd) * norm_g.astype(F32)
    y = o * jax.nn.silu(g.astype(F32))
    return y.astype(pb.dtype), s_new

def short_conv(pc, buf, conv_w):
    bg, cg, xv = jnp.split(pc, 3, axis=-1)
    z = cg * xv
    zpad = jnp.concatenate([buf.astype(z.dtype), z], axis=1)
    y = bg * causal_depthwise(zpad, conv_w)
    return y, zpad[:, -(CONV_C_W - 1):]

def fox_project(pd, b_f):
    bsz, length, _ = pd.shape
    hd = H_D * DH_D
    q = pd[..., :hd].reshape(bsz, length, H_D, DH_D)
    k = pd[..., hd:2 * hd].reshape(bsz, length, H_D, DH_D)
    v = pd[..., 2 * hd:3 * hd].reshape(bsz, length, H_D, DH_D)
    logf = jax.nn.log_sigmoid((pd[..., 3 * hd:] + b_f).astype(F32))
    return q, k, v, logf

def fox_prompt(q, k, v, logf):
    bsz, length, nh, dh = q.shape
    nb = length // Q_BLOCK
    c_keys = jnp.cumsum(logf, axis=1).transpose(0, 2, 1)
    q_blocks = q.reshape(bsz, nb, Q_BLOCK, nh, dh).swapaxes(0, 1)
    c_blocks = c_keys.reshape(bsz, nh, nb, Q_BLOCK).transpose(2, 0, 1, 3)
    k_pos = jnp.arange(length)
    scale = dh ** -0.5

    def one_block(args):
        blk, qb, cb = args
        s = jnp.einsum('bqhd,bkhd->bhqk', qb, k).astype(F32) * scale
        s = s + cb[..., :, None] - c_keys[:, :, None, :]
        q_pos = blk * Q_BLOCK + jnp.arange(Q_BLOCK)
        s = jnp.where(k_pos[None, :] <= q_pos[:, None], s, NEG_INF)
        p = jax.nn.softmax(s, axis=-1).astype(v.dtype)
        return jnp.einsum('bhqk,bkhd->bqhd', p, v)

    o = lax.map(one_block, (jnp.arange(nb), q_blocks, c_blocks))
    return o.swapaxes(0, 1).reshape(bsz, length, nh * dh)

def fox_decode(q, k, v, logf, k_past, v_past, logf_past):
    bsz, t_new, nh, dh = q.shape
    p_len = k_past.shape[1]
    scale = dh ** -0.5
    c_past = jnp.cumsum(logf_past.astype(F32), axis=1)
    c_new = jnp.cumsum(logf, axis=1).transpose(0, 2, 1)
    tail = (c_past[:, -1:] - c_past).transpose(0, 2, 1)
    bias_past = c_new[..., :, None] + tail[:, :, None, :]
    bias_new = c_new[..., :, None] - c_new[..., None, :]
    causal = jnp.tril(jnp.ones((t_new, t_new), bool))
    s_past = jnp.einsum('bthd,bshd->bhts', q, k_past.astype(q.dtype)).astype(F32) * scale + bias_past
    s_new = jnp.einsum('bthd,bshd->bhts', q, k).astype(F32) * scale + bias_new
    s_new = jnp.where(causal, s_new, NEG_INF)
    p = jax.nn.softmax(jnp.concatenate([s_past, s_new], axis=-1), axis=-1).astype(v.dtype)
    o = (jnp.einsum('bhts,bshd->bthd', p[..., :p_len], v_past.astype(v.dtype))
         + jnp.einsum('bhts,bshd->bthd', p[..., p_len:], v))
    return o.reshape(bsz, t_new, nh * dh)

def decoder_layer(x, lw, conv_a_buf, gla_state, conv_c_buf, fox_past):
    (f1_pre, f1_post, f1_wg, f1_wu, f1_wd, m_pre, m_post, w_in, w_out,
     a_cw, a_cb, a_lg, a_lb, b_wa2, b_ba, b_ng, c_cw, d_bf,
     f2_pre, f2_post, f2_wg, f2_wu, f2_wd) = lw
    bsz, length, _ = x.shape
    h = x + 0.5 * rms_norm(swiglu(rms_norm(x, f1_pre), f1_wg, f1_wu, f1_wd), f1_post)
    u = rms_norm(h, m_pre)
    p_all = u @ w_in
    ya, buf_a = conformer_conv(p_all[..., OFF_A:OFF_B], conv_a_buf, a_cw, a_cb, a_lg, a_lb)
    yb, s_b = gla_mixer(p_all[..., OFF_B:OFF_C], gla_state, b_wa2, b_ba, b_ng)
    yc, buf_c = short_conv(p_all[..., OFF_C:OFF_D], conv_c_buf, c_cw)
    q, k, v, logf = fox_project(p_all[..., OFF_D:N_IN], d_bf)
    if fox_past is None:
        yd = fox_prompt(q, k, v, logf)
    else:
        yd = fox_decode(q, k, v, logf, fox_past[0], fox_past[1], fox_past[2])
    y = jnp.concatenate([ya, yb, yc, yd], axis=-1) @ w_out
    h = h + rms_norm(y, m_post)
    h = h + 0.5 * rms_norm(swiglu(rms_norm(h, f2_pre), f2_wg, f2_wu, f2_wd), f2_post)
    return h, (buf_a, s_b, buf_c, k, v, logf)

def setup_inputs(seed: int = 0) -> dict:
    key = jax.random.key(seed)
    ks = jax.random.split(key, 40)
    n_pages = PAST_LEN // PAGE_SIZE
    n_used = DEC_BATCH * n_pages
    n_pool = n_used + max(1, n_used // 4)

    def nrm(k, shape, scale):
        return scale * jax.random.normal(k, shape, F32)

    def gain(k, shape):
        return 1.0 + 0.05 * jax.random.normal(k, shape, F32)

    page_table = jax.random.permutation(ks[8], n_pool)[:n_used].reshape(DEC_BATCH, n_pages).astype(jnp.int32)
    return {
        'x_prompt': nrm(ks[0], (BATCH, SEQ, D_MODEL), 1.0),
        'x_sample': nrm(ks[1], (DEC_BATCH, DEC_SEQ, D_MODEL), 1.0),
        'state_conv_a': nrm(ks[2], (DEPTH, DEC_BATCH, CONV_A_W - 1, C_A), 0.5),
        'state_gla': nrm(ks[3], (DEPTH, DEC_BATCH, H_B, DK_B, DV_B), 0.5),
        'state_conv_c': nrm(ks[4], (DEPTH, DEC_BATCH, CONV_C_W - 1, C_C), 0.5),
        'cache_k': nrm(ks[5], (DEPTH, n_pool, PAGE_SIZE, H_D, DH_D), 1.0),
        'cache_v': nrm(ks[6], (DEPTH, n_pool, PAGE_SIZE, H_D, DH_D), 1.0),
        'cache_logf': jax.nn.log_sigmoid(FORGET_BIAS_INIT + jax.random.normal(ks[7], (DEPTH, n_pool, PAGE_SIZE, H_D), F32)),
        'page_table': page_table,
        'ffn1_pre_g': gain(ks[9], (DEPTH, D_MODEL)),
        'ffn1_post_g': gain(ks[10], (DEPTH, D_MODEL)),
        'ffn1_w_gate': nrm(ks[11], (DEPTH, D_MODEL, D_FF), D_MODEL ** -0.5),
        'ffn1_w_up': nrm(ks[12], (DEPTH, D_MODEL, D_FF), D_MODEL ** -0.5),
        'ffn1_w_down': nrm(ks[13], (DEPTH, D_FF, D_MODEL), D_FF ** -0.5),
        'mix_pre_g': gain(ks[14], (DEPTH, D_MODEL)),
        'mix_post_g': gain(ks[15], (DEPTH, D_MODEL)),
        'w_in': nrm(ks[16], (DEPTH, D_MODEL, N_IN), D_MODEL ** -0.5),
        'w_out': nrm(ks[17], (DEPTH, D_MIX, D_MODEL), D_MIX ** -0.5),
        'a_conv_w': nrm(ks[18], (DEPTH, CONV_A_W, C_A), CONV_A_W ** -0.5),
        'a_conv_b': nrm(ks[19], (DEPTH, C_A), 0.02),
        'a_ln_g': gain(ks[20], (DEPTH, C_A)),
        'a_ln_b': nrm(ks[21], (DEPTH, C_A), 0.02),
        'b_gate_w2': nrm(ks[22], (DEPTH, GLA_RANK, H_B * DK_B), GLA_RANK ** -0.5),
        'b_gate_b': nrm(ks[23], (DEPTH, H_B * DK_B), 0.1),
        'b_out_norm_g': gain(ks[24], (DEPTH, H_B * DV_B)),
        'c_conv_w': nrm(ks[25], (DEPTH, CONV_C_W, C_C), CONV_C_W ** -0.5),
        'd_forget_b': FORGET_BIAS_INIT + nrm(ks[26], (DEPTH, H_D), 0.1),
        'ffn2_pre_g': gain(ks[27], (DEPTH, D_MODEL)),
        'ffn2_post_g': gain(ks[28], (DEPTH, D_MODEL)),
        'ffn2_w_gate': nrm(ks[29], (DEPTH, D_MODEL, D_FF), D_MODEL ** -0.5),
        'ffn2_w_up': nrm(ks[30], (DEPTH, D_MODEL, D_FF), D_MODEL ** -0.5),
        'ffn2_w_down': nrm(ks[31], (DEPTH, D_FF, D_MODEL), D_FF ** -0.5),
    }

def reference(x_prompt, x_sample, state_conv_a, state_gla, state_conv_c, cache_k, cache_v, cache_logf,
              page_table, ffn1_pre_g, ffn1_post_g, ffn1_w_gate, ffn1_w_up, ffn1_w_down, mix_pre_g,
              mix_post_g, w_in, w_out, a_conv_w, a_conv_b, a_ln_g, a_ln_b, b_gate_w2, b_gate_b,
              b_out_norm_g, c_conv_w, d_forget_b, ffn2_pre_g, ffn2_post_g, ffn2_w_gate, ffn2_w_up,
              ffn2_w_down):
    bp = x_prompt.shape[0]
    bd = page_table.shape[0]
    hp, hs = x_prompt, x_sample
    p_ca, p_gla, p_cc, p_k, p_v, p_lf = [], [], [], [], [], []
    s_ca, s_gla, s_cc, s_k, s_v, s_lf = [], [], [], [], [], []
    for l in range(DEPTH):
        lw = (ffn1_pre_g[l], ffn1_post_g[l], ffn1_w_gate[l], ffn1_w_up[l], ffn1_w_down[l],
              mix_pre_g[l], mix_post_g[l], w_in[l], w_out[l],
              a_conv_w[l], a_conv_b[l], a_ln_g[l], a_ln_b[l],
              b_gate_w2[l], b_gate_b[l], b_out_norm_g[l], c_conv_w[l], d_forget_b[l],
              ffn2_pre_g[l], ffn2_post_g[l], ffn2_w_gate[l], ffn2_w_up[l], ffn2_w_down[l])
        hp, st = decoder_layer(
            hp, lw,
            jnp.zeros((bp, CONV_A_W - 1, C_A), hp.dtype),
            jnp.zeros((bp, H_B, DK_B, DV_B), F32),
            jnp.zeros((bp, CONV_C_W - 1, C_C), hp.dtype),
            None)
        p_ca.append(st[0]); p_gla.append(st[1]); p_cc.append(st[2])
        p_k.append(st[3]); p_v.append(st[4]); p_lf.append(st[5])
        k_past = cache_k[l][page_table].reshape(bd, -1, H_D, DH_D)
        v_past = cache_v[l][page_table].reshape(bd, -1, H_D, DH_D)
        lf_past = cache_logf[l][page_table].reshape(bd, -1, H_D)
        hs, st = decoder_layer(hs, lw, state_conv_a[l], state_gla[l], state_conv_c[l],
                               (k_past, v_past, lf_past))
        s_ca.append(st[0]); s_gla.append(st[1]); s_cc.append(st[2])
        s_k.append(st[3]); s_v.append(st[4]); s_lf.append(st[5])
    return (hp, hs,
            jnp.stack(p_ca), jnp.stack(p_gla), jnp.stack(p_cc), jnp.stack(p_k), jnp.stack(p_v), jnp.stack(p_lf),
            jnp.stack(s_ca), jnp.stack(s_gla), jnp.stack(s_cc), jnp.stack(s_k), jnp.stack(s_v), jnp.stack(s_lf))


_drawn_inputs = setup_inputs


def setup_inputs(seed=0):
    import zlib

    import numpy as np

    out = dict(_drawn_inputs(seed))
    spreads = {}
    factors = {'a_conv_b': 2.769, 'a_ln_b': 5.157}
    for name, (base, spread) in spreads.items():
        noise = np.random.default_rng([zlib.crc32(name.encode()), seed]).standard_normal(out[name].shape)
        drawn = base * np.exp(spread * noise) if base else spread * noise
        out[name] = __import__('jax').numpy.asarray(drawn.astype(out[name].dtype))
    for name, factor in factors.items():
        out[name] = (out[name] * factor).astype(out[name].dtype)
    return out
```

```python
from contextlib import ExitStack

import concourse.bass as bass
from concourse import mybir

F32 = mybir.dt.float32
F32R = mybir.dt.float32r
I32 = mybir.dt.int32
ALU = mybir.AluOpType
ACT = mybir.ActivationFunctionType
AX = mybir.AxisListType

P = 128
L = 2
D = 1024
TP, TD = 256, 8
NT = TP + TD
KD = D // P
FF = 2816
KF = FF // P
NPOOL, PAGE, NPAGES = 20, 128, 2
EPS = 1e-6
LN_HALF = -0.6931471805599453
TAPS_A, TAPS_C = 31, 3
H = 4
DK, DV, CH = 32, 64, 64
GLA_TAU = 16.0
COLS = KD * P

ALR, FG, BQ, BK, AV, AG, BG, BV, DQ, DKK, DVV, CB, CC, CX = 0, 1, 2, 3, 4, 6, 8, 10, 12, 14, 16, 18, 20, 22
IN_WIDTH = [16, 4] + [P] * 22

RING = 4
PHASES = {"gu0": (0, 44), "dn0": (44, 24), "in": (68, 24), "out": (92, 8), "gu1": (100, 44), "dn1": (144, 24)}
ORDER = list(PHASES)
UNITS = 168
GROUP = 3
LEAD = 3
DN_TILES = [8, 8, 6]

PAR = {}
_at = 0
for _n, _w in (("pre", 24), ("post", 24), ("acw", 62), ("acb", 2), ("alg", 2), ("alb", 2), ("ba", 1),
               ("bng", 2), ("ccw", 6), ("bf", 1), ("wa2", P)):
    PAR[_n] = _at
    _at += _w
NPAR = _at

CON = {}
_at = 0
for _n, _w in (("ident", 128), ("ones", TP), ("blk", 128), ("tri", 3 * P), ("lvm", 7 * CH), ("rst", TP),
               ("hv", H * DV), ("hvt", 2 * P), ("sel", H * P), ("heads", 2 * P), ("dec", TD)):
    CON[_n] = _at
    _at += _w
NCON = _at
LEVELS = [0, 32, 16, 8, 4, 2, 1]

YB, YA, YD, YC = 0, 2, 4, 6

PATTERN = {"gu0": 4, "dn0": 12, "in": 24, "out": 8, "gu1": 4, "dn1": 12}
PAST = 16 * (5 + TD * NPAGES)
INIT = {"split_done": RING, "unit_done": RING, "gu_read": 4, "y_scaled": 2, "silu_ready": 2, "act_ready": 2, "act_lo": 2,
        "hg_hi": 8, "h_sq": 8, "h_acc": 9, "hg_ready": 8, "y_acc": 1, "y_sum": 1, "stored": 1}


def decoder_kernel(nc, ins, outs, per, tally):
    with ExitStack() as ctx:
        def sb(name, shape, dt=F32, scope=ctx):
            return scope.enter_context(nc.sbuf_tensor(name, shape, dt))

        resid = sb("resid", [P, KD, NT])
        hg_hi = sb("hg_hi", [P, KD, NT], F32R)
        hg_lo = sb("hg_lo", [P, KD, NT], F32R)
        yg = sb("yg", [P, KD, NT])
        ymix = yg
        raw = sb("raw", [P, RING, COLS])
        w_hi = sb("w_hi", [P, RING, COLS], F32R)
        w_lo = sb("w_lo", [P, RING, COLS], F32R)
        par_all = sb("par_all", [P, L, NPAR])
        par = sb("par", [P, NPAR])
        gain0 = sb("gain0", [P, KD])
        con = sb("con", [P, NCON])
        biases = sb("biases", [P, 3])
        rs_y = sb("rs_y", [P, NT])
        rs_h = sb("rs_h", [P, NT])
        ln_t = sb("ln_t", [P, NT])
        y_acc = sb("y_acc", [P, NT])
        h_acc = sb("h_acc", [P, NT])
        y_sq = sb("y_sq", [P, 2, NT])
        h_sq = sb("h_sq", [P, 2, NT])
        z_t = sb("z_t", [P, 2, NT])
        with ExitStack() as scope:
            act_hi = sb("act_hi", [P, KF, NT], F32R, scope)
            act_lo = sb("act_lo", [P, KF, NT], F32R, scope)
            gate_s = sb("gate_s", [P, 2, NT], F32, scope)
            up_s = sb("up_s", [P, 2, NT], F32, scope)
            silu_s = sb("silu_s", [P, 2, NT], F32, scope)
            act_s = sb("act_s", [P, 2, NT], F32, scope)
        proj = sb("proj", [P, 24, NT])
        ym_hi = sb("ym_hi", [P, KD, NT], F32R)
        ym_lo = sb("ym_lo", [P, KD, NT], F32R)
        lv = sb("lv", [P, 6, TP])
        lvf = lv[:, :, :].rearrange("p a b -> p (a b)")
        o_sq = lvf[:, 0:2 * NT].rearrange("p (a b) -> p a b", a=2)
        o_rs = lvf[:, 2 * NT:4 * NT].rearrange("p (a b) -> p a b", a=2)
        c_tmp = o_sq
        with ExitStack() as scope:
            q_heads = sb("q_heads", [P, H, TP], F32, scope)
            q_lv = sb("q_lv", [P, H, TP], F32, scope)
            scores = sb("scores", [P, 512], F32, scope)
            level = sb("level", [P, 512], F32, scope)
        sm = sb("sm", [P, H, 3 * P])
        smT = sb("smT", [P, H, 3 * P])
        smT_flat = smT[:, :, :].rearrange("p a b -> p (a b)")
        a_prod = smT_flat[:, 0:2 * TD * TAPS_A].rearrange("p (c b t) -> p c b t", c=2, b=TD)
        lft = smT[0:H, 3, 0:NT]
        vtok = sb("vtok", [P, 2, TP])
        kdt = sb("kdt", [P, 2, P])
        state = sb("state", [P, H, H * DV])
        v_diag = state[:, :, :].rearrange("p a (b v) -> p (a b) v", v=DV)
        st_tmp = sb("st_tmp", [P, TD, DV])
        sg = sb("sg", [P, 2, NT])
        a_pad = sb("a_pad", [P, 2, TAPS_A - 1 + TP])
        qm = sb("qm", [P, H, NT])
        tail = sb("tail", [H * TD, TP])
        sd = sb("sd", [H * TD, TP + 1])
        sct = sb("sct", [P, 64])
        pm = sb("pm", [P, H, TD])
        ptd = sb("ptd", [P, 2, H, TD])
        p_new = sb("p_new", [H * TD, TD])
        stats = sb("stats", [P, 3, 8])
        dstat = sb("dstat", [H * TD, 4])
        d_tmp = sb("d_tmp", [P, 16])
        a_dec = sb("a_dec", [P, 2, TD, TAPS_A])
        z_dec = sb("z_dec", [P, 2, TD, TAPS_C])
        st = sb("st", [P, TD, DV])
        lfp = sb("lfp", [H * TD, TP])
        lfn = sb("lfn", [H * TD, 1])
        pages = sb("pages", [P, 16, TP])
        table = sb("table", [1, TD * NPAGES], I32)
        z_pad = lvf[:, 2 * NT:2 * NT + 2 * (TP + 2)].rearrange("p (a b) -> p a b", a=2)
        la, bc = z_t[:, 0, :], z_t[:, 1, :]
        soft, eb = h_sq[:, 0, :], h_sq[:, 1, :]
        a_rs = h_sq[:, 0, :]
        a_sqr = sg
        lf, cf = y_sq[0:H, 0, :], y_sq[0:H, 1, :]

        ub = [ctx.enter_context(nc.psum_tensor(f"ub{i}", [P, 512], F32)) for i in range(4)]
        mb = [ctx.enter_context(nc.psum_tensor(f"mb{i}", [P, 512], F32)) for i in range(4, 8)]
        NORM = mb[3][:, 0:NT]

        S = {n: ctx.enter_context(nc.semaphore(n)) for n in per}
        landed = [ctx.enter_context(nc.semaphore(f"landed{i}")) for i in range(RING)]
        x_in = [ctx.enter_context(nc.semaphore(f"x_in{k}")) for k in range(KD)]
        setup = ctx.enter_context(nc.semaphore("setup"))
        started = ctx.enter_context(nc.semaphore("started"))

        def sig(name, times=1, n=1):
            tally[name] = tally.get(name, 0) + n * times
            return S[name], n

        def at(l, name, k):
            assert not isinstance(k, int) or k + INIT.get(name, 0) > 0, (name, k)
            return S[name], l * per[name] + k + INIT.get(name, 0)

        def const(name, cols, part=P):
            return con[0:part, CON[name]:CON[name] + cols]

        ident, ones, blk = const("ident", P), const("ones", P), const("blk", P)

        def tile_of(tiles, n):
            return tiles[:, n, :] if isinstance(n, int) else tiles[:, bass.ds(n, 1), :].rearrange("p a c -> p (a c)")

        def steps(eng, phase, l, body, pattern=4, peel_first=False):
            first, n = PHASES[phase]
            turns = n // pattern

            def turn(i, reps):
                for s in range(pattern):
                    idx, ph, row = i * pattern + s + LEAD, phase, l
                    if reps == 1 and idx >= n:
                        ph, idx = ORDER[(ORDER.index(phase) + 1) % len(ORDER)], idx - n
                        row = l + 1 if phase == "dn1" else l
                    width = DN_TILES[(s + LEAD) % 3] * P if ph.startswith("dn") else COLS
                    if ph.startswith("dn") and ph != phase:
                        width = DN_TILES[idx % 3] * P
                    if ph == "in":
                        width = KD * IN_WIDTH[idx]
                    body(i, s, reps, dict(
                        weights=ins["w_" + ph], row=row * PHASES[ph][1] + idx, width=width,
                        slot=(s + LEAD) % RING, number=l * UNITS + first + i * pattern + s + LEAD,
                        turn=l * (UNITS // RING) + first // RING + i * (pattern // RING) + (s + LEAD) // RING))
            if peel_first:
                turn(0, 1)
            if turns > 1 + peel_first:
                with eng.Fori(int(peel_first), turns - 1) as i:
                    turn(i, turns - 1 - peel_first)
            turn(turns - 1, 1)

        def load_unit(eng, lead, reps):
            row = eng.snap(lead["row"])
            eng.wait_ge(S["split_done"], lead["number"] + 1)
            eng.dma_start(raw[:, lead["slot"], 0:lead["width"]],
                          lead["weights"][bass.ds(row, 1), :, 0:lead["width"]].rearrange("a p c -> p (a c)"))\
               .then_inc(landed[lead["slot"]], 16)

        def round_unit(eng, lead, reps):
            w, slot = lead["width"], lead["slot"]
            eng.wait_ge(landed[slot], (lead["turn"] + 1) * 16)
            eng.wait_ge(S["unit_done"], lead["number"] + 1)
            eng.activation(w_hi[:, slot, 0:w], raw[:, slot, 0:w], ACT.Copy).then_inc(*sig("hi_ready", reps))

        def rest_unit(eng, lead, reps):
            w, slot = lead["width"], lead["slot"]
            eng.wait_ge(S["hi_ready"], lead["number"] + 1)
            eng.tensor_tensor(w_lo[:, slot, 0:w], raw[:, slot, 0:w], w_hi[:, slot, 0:w].bitcast(F32), ALU.subtract)\
               .then_inc(*sig("split_done", reps))

        def first_unit(s):
            return dict(weights=ins["w_gu0"], row=s, width=COLS, slot=s, number=s, turn=0)

        def multiply_unit(eng, out, slot, x_hi, x_lo, tiles, k0, first, last, reps, m=P, ready=None):
            for k in range(tiles):
                if ready:
                    ready(k0 + k)
                a_hi, a_lo = (w[:, slot, k * m:(k + 1) * m] for w in (w_hi, w_lo))
                eng.matmul(out, a_hi, x_hi[:, k0 + k, :], start=(first and k == 0), stop=False)
                eng.matmul(out, a_hi, x_lo[:, k0 + k, :], start=False, stop=False)
                mm = eng.matmul(out, a_lo, x_hi[:, k0 + k, :], start=False, stop=(last and k == tiles - 1))
            mm.then_inc(*sig("unit_done", reps))

        def unit_bank(n):
            return ub[n if n < GROUP else n % 2]

        def multiply_first(eng, l, phase, q, banks, widths):
            for k in range(KD):
                for s in range(GROUP):
                    m = widths[s]
                    if k == 0:
                        eng.wait_ge(S["split_done"], l * UNITS + PHASES[phase][0] + s + 1 + RING)
                    if s == 0:
                        eng.wait_ge(*at(l, "hg_ready", 8 * q + k - 7))
                    a_hi, a_lo = (w[:, s, k * m:(k + 1) * m] for w in (w_hi, w_lo))
                    out = banks[s][0:m, 0:NT]
                    eng.matmul(out, a_hi, hg_hi[:, k, :], start=k == 0, stop=False)
                    eng.matmul(out, a_hi, hg_lo[:, k, :], start=False, stop=False)
                    mm = eng.matmul(out, a_lo, hg_hi[:, k, :], start=False, stop=k == KD - 1)
                    if k == KD - 1:
                        mm.then_inc(*sig("unit_done"))

        block = ctx.enter_context(nc.Block())

        @block.sync
        def _(sp):
            sp.dma_start(gain0[:, :], ins["gain0"]).then_inc(x_in[0], 16)
            for k in range(KD):
                if k < LEAD:
                    sp.dma_start(raw[:, k, :], ins["w_gu0"][k, :, :]).then_inc(landed[k], 16)
                sp.dma_start(resid[:, k, :], ins["x"][:, k, :]).then_inc(x_in[k], 16)
            sp.dma_start(con[:, :], ins["con"]).then_inc(setup, 16)
            sp.dma_start(par_all[:, :, :], ins["par"]).then_inc(setup, 16)
            sp.dma_start(table[:, :], ins["table"]).then_inc(setup, 16)

            sp.wait_ge(setup, 16 * 3)

            def page_row(l, e):
                return sp.snap(l * NPOOL + sp.value_load(table[0:1, e:e + 1], min_val=0, max_val=NPOOL - 1))

            def load_past(l, s):
                def load(dst, src):
                    sp.dma_start(dst, ins[src][bass.ds(l, 1)].rearrange("a p c -> p (a c)")).then_inc(*sig("past", n=16))
                def load3(src, dst):
                    for c in range(2):
                        sp.dma_start(dst[:, c], ins[src + str(c)][bass.ds(l, 1)].rearrange("a p b t -> p (a b) t")).then_inc(*sig("past", n=16))
                if s < TD * NPAGES:
                    b, g = s // NPAGES, s % NPAGES
                    page = page_row(l, s)
                    if s == 0:
                        sp.wait_ge(*at(l, "stored", 0))
                    sp.dma_start(lfp[b:H * TD:TD, g * PAGE:(g + 1) * PAGE],
                                 ins["cache_f"][bass.ds(page, 1)].rearrange("a p c -> p (a c)")).then_inc(*sig("past", n=16))
                    sp.dma_start(pages[:, s, :], ins["cache_k"][bass.ds(page, 1)].rearrange("a p c -> p (a c)"))\
                      .then_inc(*sig("pages_in", n=16))
                if s == 16:
                    load(st[:, :, :].rearrange("p a b -> p (a b)"), "state_b")
                if s == 18:
                    load3("state_a", a_dec[:, :, :, 0:TAPS_A - 1])
                if s == 20:
                    load3("state_c", z_dec[:, :, :, 0:TAPS_C - 1])

            def load_values(l, e):
                page = page_row(l, e)
                if e % 8 == 0:
                    sp.wait_ge(*at(l, "d_dsc", e // 8 + 1))
                sp.dma_start(pages[:, e, :], ins["cache_v"][bass.ds(page, 1)].rearrange("a p c -> p (a c)"))\
                  .then_inc(*sig("pages_in", n=16))

            def store(l, name, src, **kw):
                dst = outs[name][bass.ds(l, 1)]
                sp.dma_start(dst.rearrange("a p c -> p (a c)"), src, **kw).then_inc(*sig("stored", n=16))

            def store_states(l):
                sp.wait_ge(*at(l, "a_in", 2))
                store(l, "kv", proj[:, DKK:DKK + 4, :].rearrange("p a b -> p (a b)"))
                for c in range(2):
                    store(l, f"pa{c}", a_pad[:, c, TP:TP + TAPS_A - 1])
                    sp.dma_start(outs[f"sa{c}"][bass.ds(l, 1)].rearrange("a p b t -> p (a b) t"), a_dec[:, c, :, 1:TAPS_A])\
                      .then_inc(*sig("stored", n=16))
                sp.wait_ge(*at(l, "b_S", 3))
                for h in range(H):
                    store(l, f"pb{h}", state[h * DK:(h + 1) * DK, 3, h * DV:(h + 1) * DV])
                sp.wait_ge(*at(l, "b_sd", 1))
                store(l, "sb", st[:, :, :].rearrange("p a b -> p (a b)"))
                sp.wait_ge(*at(l, "c_z", 3))
                sp.dma_start(outs["pc"][bass.ds(l, 1)].rearrange("a p c t -> p (a c) t"), z_pad[:, :, TP:TP + 2]).then_inc(*sig("stored", n=16))
                for c in range(2):
                    sp.dma_start(outs[f"sc{c}"][bass.ds(l, 1)].rearrange("a p b t -> p (a b) t"), z_dec[:, c, :, 1:3])\
                      .then_inc(*sig("stored", n=16))

            def mix(l, n):
                if n == 6:
                    sp.wait_ge(*at(l, "d_lf", 2))
                    store(l, "pf", lf[:, 0:TP])
                    sp.dma_start(outs["sf"][bass.ds(l, 1)].rearrange("a (h b) o -> h (a b o)", h=H), lf[:, TP:NT])\
                      .then_inc(*sig("stored", n=16))
                if n == 10:
                    sp.wait_ge(*at(l, "stored", 32))
                    sp.dma_start(lfn[:, :], outs["sf"][bass.ds(l, 1)].rearrange("a p o -> p (a o)"), allow_slow_non_contiguous=True)\
                      .then_inc(*sig("lfn_in", n=16))
                if n >= 16:
                    for e in (2 * (n - 16), 2 * (n - 16) + 1):
                        load_values(l, e)

            with sp.Fori(0, L) as l:
                for phase in ORDER:
                    def turn(i, s, reps, lead):
                        load_unit(sp, lead, reps)
                        if phase == "dn0":
                            load_past(l, s)
                        if phase == "in":
                            mix(l, s)
                        if phase == "out" and s == 2:
                            store_states(l)
                    steps(sp, phase, l, turn, 24 if phase == "dn0" else PATTERN[phase])
            sp.wait_ge(S["stored"], L * per["stored"] + INIT["stored"])
            for k in range(KD):
                sp.wait_ge(*at(L - 1, "h_ready", 16 + k + 1))
                sp.dma_start(outs["h"][:, k, :], resid[:, k, :]).then_inc(setup, 16)
            sp.wait_ge(setup, 16 * (3 + KD))

        @block.tensor
        def _(pe):
            def feed_forward(l, q):
                f = q // 2
                gu, dn = f"gu{f}", f"dn{f}"

                def gate_up(i, s, reps):
                    t = i * 4 + s
                    pe.wait_ge(S["split_done"], l * UNITS + PHASES[gu][0] + t + 1 + RING)
                    pe.wait_ge(*at(l, "gu_read", f * 44 + t - 3))
                    multiply_unit(pe, ub[s][:, 0:NT], s, hg_hi, hg_lo, KD, 0, True, True, reps)

                pe.wait_ge(*at(l, "gu_read", f * 44))
                multiply_first(pe, l, gu, q, ub, [P] * GROUP)
                pe.wait_ge(setup, 16 * 3)
                pe.wait_ge(*at(l, "h_acc", 9 * q))
                pe.matmul(NORM, ones, h_acc[:, :], start=True, stop=True).then_inc(*sig("h_sum"))
                gate_up(0, 3, 1)
                with pe.Fori(0, 2) as i:
                    for s in range(20):
                        gate_up(i * 5 + s // 4 + 1, s % 4, 2)
                pe.wait_ge(*at(l, "gu_read", f * 44 + 42))

                def down(i, s, reps):
                    n, part = i * 4 + s // 3, s % 3
                    pe.wait_ge(S["split_done"], l * UNITS + PHASES[dn][0] + i * 12 + s + 1 + RING)
                    if part == 0:
                        pe.wait_ge(*at(l, "y_scaled", q * 8 + n - 1))
                    multiply_unit(pe, ub[s // 3 % 2][:, 0:NT], s % RING, act_hi, act_lo, DN_TILES[part], 8 * part,
                                  part == 0, part == 2, reps,
                                  ready=(lambda k: pe.wait_ge(*at(l, "act_lo", f * 22 + k + 1))) if s < 3 and reps == 1 else None)
                for s in range(12):
                    down(0, s, 1)
                for s in range(12):
                    down(1, s, 1)
                output_norm(l, q)

            def output_norm(l, q):
                pe.wait_ge(*at(l, "y_acc", 8 * q + 8))
                pe.matmul(NORM, ones, y_acc[:, :], start=True, stop=False)
                pe.wait_ge(*at(l, "y_sq", 8 * q + 8))
                pe.matmul(NORM, ones, y_sq[:, 1, :], start=False, stop=True).then_inc(*sig("y_sum"))

            def after(l, **counts):
                pe.wait_ge(setup, 16 * 3)
                for name, k in counts.items():
                    pe.wait_ge(*at(l, name, k))

            def rows(i):
                return slice(CH * i, CH * (i + 1))

            def gla_level(l, i):
                if i == 0:
                    after(l, b_qb0=1)
                    k_in, q_in = proj[:, BK, :], q_heads
                else:
                    after(l, b_kt=i, b_qbl=i)
                    k_in, q_in = lv[:, 4 + i % 2, :], q_lv
                if i >= 2:
                    after(l, b_msk=i - 1)
                for c in range(4):
                    mm = pe.matmul(ub[2 + i % 2][rows(c % 2), (c // 2) * TP:(c // 2 + 1) * TP], k_in[:, c * CH:(c + 1) * CH],
                                   q_in[:, :, c * CH:(c + 1) * CH], start=True, stop=True)
                mm.then_inc(*sig("b_sc"))

            def transposes(bank, src, name):
                for g in range(2):
                    for j in range(2):
                        mm = pe.transpose(bank[:, (2 * g + j) * P:(2 * g + j + 1) * P], src[:, j, g * P:(g + 1) * P], ident)
                mm.then_inc(*sig(name))

            def gla_tokens(l):
                after(l, proj=12)
                transposes(mb[0], proj[:, BV:BV + 2, :], "b_vT")
                after(l, b_kt=7)
                for g in range(2):
                    mm = pe.transpose(mb[1][:, g * P:(g + 1) * P], lv[:, 5, g * P:(g + 1) * P], ident)
                mm.then_inc(*sig("b_kdT"))

            def gla_updates(l):
                after(l, b_vx=2)
                for j in range(2):
                    mm = pe.matmul(mb[2][:, :], const("hvt", P * 2)[:, j * P:(j + 1) * P], v_diag[:, j * TD:(j + 1) * TD, :], start=j == 0, stop=j == 1)
                mm.then_inc(*sig("b_vb"))
                after(l, b_vt=1, b_kdt=1, b_msk=7)
                for c in range(4):
                    mm = pe.matmul(ub[2 + c % 2][:, (c // 2) * TP:(c // 2 + 1) * TP], kdt[rows(c % 2), c // 2, :], vtok[rows(c % 2), c // 2, :],
                                   start=True, stop=True)
                mm.then_inc(*sig("b_kv"))

            def gla_outputs(l):
                after(l, b_S=3, b_asc=6, b_qe=1)
                qe = proj[:, BQ, :]
                for c in (1, 0, 3, 2):
                    for j in range(2):
                        out = mb[c % 2][:, (c // 2 * 2 + j) * CH:(c // 2 * 2 + j + 1) * CH]
                        if c:
                            pe.matmul(out, state[:, c - 1, j * P:(j + 1) * P], qe[:, c * CH:(c + 1) * CH], start=True, stop=False)
                        for i in range(2):
                            h = 2 * j + i
                            mm = pe.matmul(out[rows(i), :], vtok[rows(c % 2), c // 2, h * DV:(h + 1) * DV],
                                           scores[rows(c % 2), (c // 2 * H + h) * CH:(c // 2 * H + h + 1) * CH], start=c == 0, stop=True)
                mm.then_inc(*sig("b_o"))
                after(l, b_prod=1)
                for b in range(TD):
                    for i in range(2):
                        mm = pe.matmul(mb[2][rows(i), 2 * b:2 * b + 2], st_tmp[:, b, :], const("hv", H * DV)[:, i * DV::2 * DV], start=True, stop=True)
                mm.then_inc(*sig("b_od"))

            def gla_norm(l):
                after(l, b_osq=1)
                for j in range(2):
                    mm = pe.matmul(ub[2 + j][:, 0:NT], blk, o_sq[:, j, :], start=True, stop=True)
                mm.then_inc(*sig("b_gn"))

            def conv_sum(l):
                after(l, a_tap=62, a_db=1, b_rs=4)
                for c in range(2):
                    mm = pe.matmul(ub[2][:, 0:NT], ones, ymix[:, YA + c, :], start=c == 0, stop=c == 1)
                mm.then_inc(*sig("a_sum"))

            def conv_var(l):
                after(l, a_sq=1)
                for c in range(2):
                    mm = pe.matmul(ub[3][:, 0:NT], ones, a_sqr[:, c, :], start=c == 0, stop=c == 1)
                mm.then_inc(*sig("a_var"))

            def fox_scores(l, h):
                after(l, d_qm=2, d_cf=2, proj=16, b_og=3)
                if h >= 2:
                    after(l, d_sm=h - 1)
                for out, q0, n in ((mb[h % 2][:, 0:P], 0, P), (mb[h % 2][:, P:3 * P], P, TP)):
                    pe.matmul(out, qm[:, h, q0:q0 + P], proj[:, DKK + h // 2, 0:n], start=True, stop=False)
                    mm = pe.matmul(out, const("sel", H * P, H)[:, h * P:(h + 1) * P], cf[:, 0:n], start=False, stop=True)
                mm.then_inc(*sig("d_sc"))

            def fox_transposes(l, h):
                after(l, d_pn=2)
                if h >= 2:
                    after(l, d_pt=h - 1)
                for i in range(3):
                    mm = pe.transpose(mb[h % 2][:, i * P:(i + 1) * P], sm[:, h, i * P:(i + 1) * P], ident)
                mm.then_inc(*sig("d_pT"))

            def fox_outputs(l):
                after(l, d_pt=4, d_vt=1)
                for h in range(H):
                    out = mb[2][rows(h % 2), h // 2 * TP:(h // 2 + 1) * TP]
                    pe.matmul(out, vtok[:, 0, h * DV:(h + 1) * DV], smT[:, h, 0:TP], start=True, stop=False)
                    mm = pe.matmul(out[:, P:TP], vtok[:, 1, h * DV:(h + 1) * DV], smT[:, h, TP:3 * P], start=False, stop=True)
                mm.then_inc(*sig("d_o"))

            def decode_scores(l, group):
                after(l, d_qm=2, pages_in=128 * (group + 1))
                out = mb[3][:, 0:64].rearrange("p (g h b) -> p g h b", g=NPAGES, h=H)
                if group:
                    after(l, d_pm=2)
                    pe.matmul(mb[3][0:32, 320:321], pm[:, :, :].rearrange("p h b -> p (h b)"), ones[:, 0:1], start=True, stop=True)
                for b in range(4):
                    for j in range(2):
                        for g in range(NPAGES):
                            mm = pe.matmul(out[:, g, 2 * j:2 * j + 2, 4 * group + b], pages[:, (4 * group + b) * NPAGES + g, j * P:(j + 1) * P],
                                           qm[:, 2 * j:2 * j + 2, TP + 4 * group + b], start=True, stop=True)
                mm.then_inc(*sig("d_dsc"))

            def decode_transposes(l):
                after(l, d_scs=1)
                for g in range(NPAGES):
                    mm = pe.transpose(mb[3][0:32, 64 + g * P:64 + (g + 1) * P], sct[:, 32 * g:32 * (g + 1)], ident)
                mm.then_inc(*sig("d_dT"))

            def decode_back(l):
                after(l, d_dp=2)
                for g in range(NPAGES):
                    pe.transpose(mb[3][:, 384 + 32 * g:384 + 32 * (g + 1)], sd[:, g * PAGE:(g + 1) * PAGE], ident[0:32, 0:32])
                for j in range(2):
                    mm = pe.matmul(mb[3][:, 480 + TD * j:480 + TD * (j + 1)], const("heads", 2 * P, 32)[:, j * P:(j + 1) * P], p_new[:, :],
                                   start=True, stop=True)
                mm.then_inc(*sig("d_dpT"))

            def decode_outputs(l, group):
                after(l, d_ptd=1, pages_in=128 * (group + 3))
                for b in range(4):
                    for j in range(2):
                        col = 448 + (j * TD + 4 * group + b) * 2
                        for g in range(NPAGES):
                            mm = pe.matmul(mb[3][:, col:col + 2], pages[:, (4 * group + b) * NPAGES + g, j * P:(j + 1) * P],
                                           ptd[:, g, 2 * j:2 * j + 2, 4 * group + b], start=g == 0, stop=g == 1)
                mm.then_inc(*sig("d_dpv"))

            def mix(l, n):
                if n == 3:
                    after(l, proj=1)
                    pe.matmul(ub[3][:, 0:NT], par[0:16, PAR["wa2"]:PAR["wa2"] + P], proj[0:16, ALR, :], start=True, stop=True).then_inc(*sig("b_z"))
                if 5 <= n <= 11:
                    gla_level(l, n - 5)
                if n == 12:
                    gla_tokens(l)
                if n == 13:
                    gla_updates(l)
                if n == 15:
                    decode_scores(l, 0)
                    gla_outputs(l)
                if n == 17:
                    fox_scores(l, 0)
                    fox_scores(l, 1)
                if n == 18:
                    decode_scores(l, 1)
                    fox_scores(l, 2)
                    fox_scores(l, 3)
                    gla_norm(l)
                if n == 19:
                    decode_transposes(l)
                    after(l, proj=18, b_og=3)
                    transposes(mb[2], proj[:, DVV:DVV + 2, :], "d_vT")
                if n == 21:
                    decode_back(l)
                    fox_transposes(l, 0)
                    fox_transposes(l, 1)
                if n == 22:
                    decode_outputs(l, 0)
                    conv_sum(l)
                    fox_transposes(l, 2)
                    fox_transposes(l, 3)
                if n == 23:
                    fox_outputs(l)
                    conv_var(l)
                    decode_outputs(l, 1)

            def mixer(l):
                multiply_first(pe, l, "in", 1, ub, IN_WIDTH)
                pe.wait_ge(*at(l, "h_acc", 9))
                pe.matmul(NORM, ones, h_acc[:, :], start=True, stop=True).then_inc(*sig("h_sum"))
                for n in range(GROUP, 24):
                    pe.wait_ge(S["split_done"], l * UNITS + PHASES["in"][0] + n + 1 + RING)
                    pe.wait_ge(*at(l, "proj", n - 1))
                    multiply_unit(pe, unit_bank(n)[:, 0:NT], n % RING, hg_hi, hg_lo, KD, 0, True, True, 1)
                    mix(l, n)
                for n in range(8):
                    pe.wait_ge(S["split_done"], l * UNITS + PHASES["out"][0] + n + 1 + RING)
                    if n >= 2:
                        pe.wait_ge(*at(l, "y_scaled", 8 + n - 1))
                    multiply_unit(pe, ub[n % 2][:, 0:NT], n % RING, ym_hi, ym_lo, KD, 0, True, True, 1,
                                  ready=(lambda k: pe.wait_ge(*at(l, "ym_ready", k + 1))) if n == 0 else None)
                output_norm(l, 1)

            with pe.Fori(0, L) as l:
                feed_forward(l, 0)
                mixer(l)
                feed_forward(l, 2)

        @block.scalar
        def _(act):
            def input_tile(l, q, k, gain):
                act.activation(hg_hi[:, k, :], resid[:, k, :], ACT.Copy, scale=gain[:, k:k + 1]).then_inc(*sig("hg_hi"))
                if k >= 2:
                    act.wait_ge(*at(l, "h_acc", 9 * q + k))
                act.activation(h_sq[:, k % 2, :], resid[:, k, :], ACT.Square).then_inc(*sig("h_sq"))

            def output_tile(l, q, n, bank, b, reps):
                act.wait_ge(*at(l, "y_acc", 8 * q + n))
                act.activation(y_sq[:, b, :], bank[:, 0:NT], ACT.Square).then_inc(*sig("y_sq", reps))
                act.activation(yg[:, n, :] if isinstance(n, int) else yg[:, bass.ds(n, 1), :].rearrange("p a c -> p (a c)"),
                               bank[:, 0:NT], ACT.Copy,
                               scale=par[:, PAR["post"] + q * 8 + n:PAR["post"] + q * 8 + n + 1] if isinstance(n, int)
                               else par[:, bass.ds(PAR["post"] + q * 8 + n, 1)]).then_inc(*sig("y_scaled", reps))

            def rsqrt(l, name, k, out, total, scale, **bias):
                act.activation(ln_t[:, :], total, ACT.Ln, bias=biases[:, 0:1], scale=scale).then_inc(*sig(name))
                act.wait_ge(*at(l, name, k + 1))
                act.activation(out, ln_t[:, :], ACT.Exp, scale=-0.5, **bias).then_inc(*sig(name))

            def input_norm(l, q):
                act.wait_ge(*at(l, "h_sum", q + 1))
                rsqrt(l, "rh_ready", 2 * q, rs_h[:, :], NORM, 1.0 / D)

            def boundary(l, q):
                act.wait_ge(*at(l, "y_sum", q + 1))
                half = {} if q == 1 else {"bias": biases[:, 1:2]}
                rsqrt(l, "ry_ready", 2 * q, rs_y[:, :], NORM, 1.0 / D, **half)
                for k in range(KD):
                    act.wait_ge(*at(l, "h_ready", 8 * q + k + 1))
                    input_tile(l, q, k, par[:, PAR["pre"] + 8 * q:PAR["pre"] + 8 * q + 8])

            def feed_forward(l, q):
                f = q // 2
                gu, dn = f"gu{f}", f"dn{f}"

                def gate_up(i, s, reps, lead):
                    round_unit(act, lead, reps)
                    if isinstance(i, int) and i == 0 and s == 1:
                        input_norm(l, q)
                        act.preload_act_table(ACT.Silu)
                    if s % 2:
                        j, b = i * 2 + s // 2, s // 2
                        act.wait_ge(*at(l, "gu_read", f * 44 + 2 * j + 1))
                        act.activation(silu_s[:, b, :], gate_s[:, b, :], ACT.Silu).then_inc(*sig("silu_ready", reps))
                        if not (isinstance(i, int) and j == 0):
                            round_act(j - 1, 1 - b, reps)

                def round_act(j, b, reps):
                    act.wait_ge(*at(l, "act_ready", f * 22 + j + 1))
                    act.activation(tile_of(act_hi, j), act_s[:, b, :], ACT.Copy).then_inc(*sig("act_hi", reps))
                steps(act, gu, l, gate_up, peel_first=True)
                round_act(21, 1, 1)
                act.preload_act_table_set("natural_log_exp_and_others")

                def down(i, s, reps, lead):
                    round_unit(act, lead, reps)
                    if s % 3 == 2:
                        n, b = i * 4 + s // 3, s // 3 % 2
                        act.wait_ge(S["unit_done"], l * UNITS + PHASES[dn][0] + i * 12 + s + 1 + RING)
                        output_tile(l, q, n, ub[b], b, reps)
                steps(act, dn, l, down, 12)
                boundary(l, q)

            def after(l, **counts):
                for name, k in counts.items():
                    act.wait_ge(*at(l, name, k))

            def rows(i):
                return slice(CH * i, CH * (i + 1))

            def softplus(l, out, x, bias, name):
                act.activation(out, x, ACT.Abs, bias=bias).then_inc(*sig(name))
                after(l, **{name: 1})
                act.activation(out, out, ACT.Exp, scale=-1.0).then_inc(*sig(name))
                after(l, **{name: 2})
                act.activation(out, out, ACT.Ln, bias=biases[0:out.shape[0], 2:3]).then_inc(*sig(name))

            def level_decays(l, i):
                after(l, b_D=2 * i if i < 7 else 13)
                if i >= 3:
                    after(l, b_kt=i - 2, b_qbl=i - 2)
                act.activation(lv[:, 2 + i % 2, :], lv[:, i % 2, :], ACT.Exp, scale=1 / GLA_TAU).then_inc(*sig("b_E"))

            def mix(l, n):
                if n == 2:
                    after(l, b_z=1)
                    softplus(l, soft[:, :], ub[3][:, 0:NT], par[:, PAR["ba"]:PAR["ba"] + 1], "b_sp")
                if n == 3:
                    after(l, proj=2)
                    softplus(l, lft[:, :], proj[0:H, FG, :], par[0:H, PAR["bf"]:PAR["bf"] + 1], "d_sp")
                    after(l, proj=3)
                    act.activation(proj[:, BQ, :], proj[:, BQ, :], ACT.Copy, scale=DK ** -0.5).then_inc(*sig("b_qs"))
                if n == 4:
                    after(l, b_bc=2)
                    act.activation(eb[:, :], bc[:, :], ACT.Exp, scale=1 / GLA_TAU).then_inc(*sig("b_eb"))
                    level_decays(l, 1)
                if 5 <= n <= 10:
                    level_decays(l, n - 3)
                if n == 11:
                    act.preload_act_table(ACT.Sigmoid)
                    after(l, proj=10)
                    act.activation(proj[:, AG:AG + 2, :], proj[:, AG:AG + 2, :], ACT.Sigmoid).then_inc(*sig("a_sg"))
                    act.activation(sg[:, :, :], proj[:, BG:BG + 2, :], ACT.Sigmoid).then_inc(*sig("b_sg"))
                    act.preload_act_table_set("natural_log_exp_and_others")
                if n == 12:
                    after(l, b_vT=1)
                    act.activation(vtok[:, :, :].rearrange("p a b -> p (a b)"), mb[0][:, :], ACT.Copy).then_inc(*sig("b_vt"))
                    after(l, b_kdT=1)
                    act.activation(kdt[:, :, :].rearrange("p a b -> p (a b)"), mb[1][:, 0:TP], ACT.Copy).then_inc(*sig("b_kdt"))
                if n == 14:
                    after(l, proj=14, d_qz=1)
                    for i in range(2):
                        act.activation(qm[rows(i), i::2, :], proj[rows(i), DQ:DQ + 2, :], ACT.Copy).then_inc(*sig("d_qm"))
                if n == 16:
                    after(l, b_o=1)
                    o = ymix[:, YB:YB + 2, 0:TP].rearrange("p j (g c t) -> p j g c t", g=2, c=2)
                    for c in range(2):
                        act.activation(o[:, :, :, c, :].rearrange("p j g t -> p g j t"), mb[c][:, 0:TP].rearrange("p (g j t) -> p g j t", g=2, j=2),
                                       ACT.Copy).then_inc(*sig("b_og"))
                    after(l, b_od=1)
                    act.activation(ymix[:, YB:YB + 2, TP:NT], mb[2][:, 0:16].rearrange("p (b j) -> p j b", j=2), ACT.Copy).then_inc(*sig("b_og"))
                if n == 17:
                    after(l, b_og=3, b_kdT=1)
                    act.activation(o_sq[:, :, :], ymix[:, YB:YB + 2, :], ACT.Square).then_inc(*sig("b_osq"))
                if n == 18:
                    after(l, d_dsc=2)
                    act.activation(sct[:, :], mb[3][:, 0:64], ACT.Copy).then_inc(*sig("d_scs"))
                if n == 19:
                    after(l, b_gn=1)
                    for j in range(2):
                        act.activation(o_rs[:, j, :], ub[2 + j][:, 0:NT], ACT.Ln, bias=biases[:, 0:1], scale=1.0 / DV).then_inc(*sig("b_rs"))
                    for j in range(2):
                        after(l, b_rs=j + 1)
                        act.activation(o_rs[:, j, :], o_rs[:, j, :], ACT.Exp, scale=-0.5).then_inc(*sig("b_rs"))
                    after(l, d_vT=1)
                    act.activation(vtok[:, :, :].rearrange("p a b -> p (a b)"), mb[2][:, :], ACT.Copy).then_inc(*sig("d_vt"))
                if n == 20:
                    after(l, d_dmx=1)
                    act.activation(sd[:, :], sd[:, :], ACT.Exp, bias=dstat[:, 1:2], accum_out=dstat[:, 2:3]).then_inc(*sig("d_dex"))
                    after(l, d_mx=2)
                    for h in range(H):
                        for b, part in ((0, slice(0, P)), (1, slice(P, 3 * P))):
                            act.activation(sm[:, h, part], sm[:, h, part], ACT.Exp, bias=stats[:, 0, b * H + h:b * H + h + 1],
                                           accum_out=stats[:, 1, b * H + h:b * H + h + 1]).then_inc(*sig("d_ex"))
                if n == 21:
                    after(l, d_dpT=1)
                    act.activation(ptd[:, :, :, :].rearrange("p g h b -> p (g h b)"), mb[3][:, 384:448], ACT.Copy).then_inc(*sig("d_ptd"))
                    for h in (0, 1):
                        probabilities(l, h)
                if n == 22:
                    after(l, a_cen=2, b_t=2)
                    act.activation(a_sqr[:, :, :], ymix[:, YA:YA + 2, :], ACT.Square).then_inc(*sig("a_sq"))
                    for h in (2, 3):
                        probabilities(l, h)
                if n == 23:
                    after(l, a_var=1)
                    act.activation(a_rs[:, :], ub[3][:, 0:NT], ACT.Ln, bias=biases[:, 0:1], scale=1.0 / 256).then_inc(*sig("a_rsd"))
                    after(l, a_rsd=1)
                    act.activation(a_rs[:, :], a_rs[:, :], ACT.Exp, scale=-0.5).then_inc(*sig("a_rsd"))
                    after(l, d_o=1)
                    act.activation(ymix[:, YD:YD + 2, 0:TP], mb[2][:, :].rearrange("p (a b) -> p a b", a=2), ACT.Copy).then_inc(*sig("d_y"))
                    act.preload_act_table(ACT.Silu)
                    after(l, a_nrm=1)
                    for c in range(2):
                        act.activation(ymix[:, YA + c, :], ymix[:, YA + c, :], ACT.Silu, scale=par[:, PAR["alg"] + c:PAR["alg"] + c + 1],
                                       bias=par[:, PAR["alb"] + c:PAR["alb"] + c + 1]).then_inc(*sig("a_y"))
                    act.preload_act_table_set("natural_log_exp_and_others")

            def probabilities(l, h):
                after(l, d_pT=h + 1)
                act.activation(smT[:, h, :], mb[h % 2][:, 0:3 * P], ACT.Copy).then_inc(*sig("d_pt"))

            def mixer(l):
                def inp(i, s, reps, lead):
                    round_unit(act, lead, reps)
                    if s == 1:
                        input_norm(l, 1)
                    mix(l, s)
                steps(act, "in", l, inp, 24)
                def outp(i, s, reps, lead):
                    n = s
                    round_unit(act, lead, reps)
                    act.wait_ge(S["unit_done"], l * UNITS + PHASES["out"][0] + n + 1 + RING)
                    output_tile(l, 1, n, ub[n % 2], n % 2, reps)
                ready = {YB: dict(b_y=1), YA: dict(a_y=2), YD: dict(d_y=1, d_dy=2), YC: dict(c_y=1)}
                for k in range(KD):
                    after(l, **ready[k - k % 2])
                    act.activation(ym_hi[:, k, :], ymix[:, k, :], ACT.Copy).then_inc(*sig("ym_hi"))
                steps(act, "out", l, outp, 8)
                boundary(l, 1)

            act.preload_act_table_set("natural_log_exp_and_others")
            act.wait_ge(started, 3)
            for k in range(KD):
                act.wait_ge(x_in[k], 16 * (1 + (k == 0)))
                if k < LEAD:
                    round_unit(act, first_unit(k), 0)
                act.activation(hg_hi[:, k, :], resid[:, k, :], ACT.Copy, scale=gain0[:, k:k + 1]).then_inc(S["hg_hi"], 1)
                if k >= 2:
                    act.wait_ge(S["h_acc"], k)
                act.activation(h_sq[:, k % 2, :], resid[:, k, :], ACT.Square).then_inc(S["h_sq"], 1)
            with act.Fori(0, L) as l:
                act.wait_ge(*at(l, "par_ready", 1))
                feed_forward(l, 0)
                mixer(l)
                feed_forward(l, 2)

        @block.vector
        def _(dve):
            def input_rest(l, q, k, gain):
                dve.wait_ge(*at(l, "hg_hi", 8 * q + k + 1))
                dve.scalar_tensor_tensor(hg_lo[:, k, :], resid[:, k, :], gain[:, k:k + 1], hg_hi[:, k, :].bitcast(F32),
                                         ALU.mult, ALU.subtract).then_inc(*sig("hg_ready"))

            def boundary(l, q):
                dve.wait_ge(*at(l, "ry_ready", 2 * q + 2))
                for k in range(KD + 2):
                    if k < KD:
                        dve.wait_ge(*at(l, "y_scaled", 8 * q + k + 1))
                        if k >= 2:
                            dve.wait_ge(*at(l, "h_ready", 8 * q + k - 1))
                        dve.tensor_tensor(z_t[:, k % 2, :], yg[:, k, :], rs_y[:, :], ALU.mult).then_inc(*sig("z_ready"))
                    if 1 <= k <= KD:
                        dve.wait_ge(*at(l, "z_ready", 8 * q + k))
                        dve.tensor_tensor(resid[:, k - 1, :], resid[:, k - 1, :], z_t[:, (k - 1) % 2, :], ALU.add)\
                           .then_inc(*sig("h_ready"))
                    if k >= 2:
                        input_rest(l, q, k - 2, par[:, PAR["pre"] + 8 * q:PAR["pre"] + 8 * q + 8])

            def feed_forward(l, q):
                f = q // 2
                gu, dn = f"gu{f}", f"dn{f}"

                def gate_up(i, s, reps, lead):
                    j, b = i * 2 + s // 2, s // 2
                    rest_unit(dve, lead, reps)
                    if s == 1:
                        dve.wait_ge(*at(l, "rh_ready", 2 * q + 2))
                    if s % 2:
                        dve.wait_ge(S["unit_done"], l * UNITS + PHASES[gu][0] + i * 4 + s + RING)
                        dve.wait_ge(*at(l, "silu_ready", f * 22 + j - 1))
                        dve.tensor_tensor(gate_s[:, b, :], ub[s - 1][:, 0:NT], rs_h[:, :], ALU.mult)\
                           .then_inc(*sig("gu_read", reps))
                        dve.wait_ge(S["unit_done"], l * UNITS + PHASES[gu][0] + i * 4 + s + 1 + RING)
                        dve.wait_ge(*at(l, "act_ready", f * 22 + j - 1))
                        dve.tensor_tensor(up_s[:, b, :], ub[s][:, 0:NT], rs_h[:, :], ALU.mult)\
                           .then_inc(*sig("gu_read", reps))
                steps(dve, gu, l, gate_up)
                steps(dve, dn, l, lambda i, s, reps, lead: rest_unit(dve, lead, reps), 12)
                boundary(l, q)

            def after(l, **counts):
                for name, k in counts.items():
                    dve.wait_ge(*at(l, name, k))

            def log_sigmoid(l, out, x, bias, minus, name):
                dve.tensor_scalar(out, x, bias, 0.0, ALU.add, ALU.min).then_inc(*sig(name))
                after(l, **{name: 1})
                dve.tensor_tensor(out, out, minus, ALU.subtract).then_inc(*sig(name))

            def level_exponents(l, i):
                if i >= 3:
                    after(l, b_E=i - 2)
                out = lv[:, i % 2, :]
                if i == 7:
                    b, out = (t.rearrange("p (n m) -> p n m", m=CH) for t in (bc[:, 0:TP], out))
                    dve.tensor_tensor(out, b[:, :, CH - 1:CH].to_broadcast([P, TP // CH, CH]), b, ALU.subtract).then_inc(*sig("b_D"))
                    return
                m = LEVELS[i]
                b, out = (t.rearrange("p (n two m) -> p n two m", two=2, m=m) for t in (bc[:, 0:TP], out))
                mid = b[:, :, 0, m - 1:m].to_broadcast([P, TP // (2 * m), m])
                dve.tensor_tensor(out[:, :, 0, :], mid, b[:, :, 0, :], ALU.subtract).then_inc(*sig("b_D"))
                dve.tensor_tensor(out[:, :, 1, :], b[:, :, 1, :], mid, ALU.subtract).then_inc(*sig("b_D"))

            def level_keys(l, i):
                after(l, b_E=i, proj=4)
                if i >= 3:
                    after(l, b_sc=i - 1)
                dve.tensor_tensor(lv[:, 4 + i % 2, :], proj[:, BK, 0:TP], lv[:, 2 + i % 2, :], ALU.mult).then_inc(*sig("b_kt"))

            def level_mask(l, i):
                after(l, b_sc=i + 1)
                if i >= 2:
                    after(l, b_asc=i - 1)
                out = (level if i else scores)[:, :].rearrange("p (a t) -> p a t", t=CH)
                mask = const("lvm", 7 * CH)[:, i * CH:(i + 1) * CH].unsqueeze(1).to_broadcast([P, 8, CH])
                dve.tensor_tensor(out, ub[2 + i % 2][:, :].rearrange("p (a t) -> p a t", t=CH), mask, ALU.mult).then_inc(*sig("b_msk"))
                if i:
                    after(l, b_msk=i + 1)
                    dve.tensor_tensor(scores[:, :], scores[:, :], level[:, :], ALU.add).then_inc(*sig("b_asc"))

            def conv_taps(l, first, last):
                for t in range(first, last):
                    for c in range(2):
                        k = 2 * t + c
                        y, x, w = ymix[:, YA + c, 0:TP], a_pad[:, c, t:t + TP], par[:, PAR["acw"] + c * TAPS_A + t:PAR["acw"] + c * TAPS_A + t + 1]
                        if t == 0:
                            dve.tensor_scalar(y, x, w, par[:, PAR["acb"] + c:PAR["acb"] + c + 1], ALU.mult, ALU.add).then_inc(*sig("a_tap"))
                        else:
                            after(l, a_tap=k - 1)
                            dve.scalar_tensor_tensor(y, x, w, y, ALU.mult, ALU.add).then_inc(*sig("a_tap"))

            def mix(l, n):
                if n == 2:
                    after(l, b_z=1)
                    log_sigmoid_b = (la[:, :], ub[3][:, 0:NT], par[:, PAR["ba"]:PAR["ba"] + 1], soft[:, :], "b_la")
                    after(l, b_sp=3)
                    log_sigmoid(l, *log_sigmoid_b)
                    after(l, b_la=2)
                    dve.tensor_tensor_scan(bc[:, 0:TP], const("rst", TP), la[:, 0:TP], 0.0, ALU.mult, ALU.add).then_inc(*sig("b_bc"))
                    dve.tensor_copy(bc[:, TP:NT], la[:, TP:NT]).then_inc(*sig("b_bc"))
                if n == 3:
                    after(l, d_sp=3, proj=2)
                    log_sigmoid(l, lf[:, :], proj[0:H, FG, :], par[0:H, PAR["bf"]:PAR["bf"] + 1], lft[:, :], "d_lf")
                    after(l, b_bc=2)
                    level_exponents(l, 1)
                    level_exponents(l, 2)
                    after(l, d_lf=2)
                    dve.tensor_tensor_scan(cf[:, 0:TP], const("ones", TP, H), lf[:, 0:TP], 0.0, ALU.mult, ALU.add).then_inc(*sig("d_cf"))
                    after(l, d_cf=1)
                    dve.tensor_scalar(cf[:, 0:TP], cf[:, 0:TP], -8.0, None, ALU.mult).then_inc(*sig("d_cf"))
                if 4 <= n <= 10:
                    if n <= 8:
                        level_exponents(l, n - 1)
                    level_keys(l, n - 3)
                if 6 <= n <= 12:
                    level_mask(l, n - 6)
                if 13 <= n <= 21:
                    if n == 13:
                        after(l, a_in=2)
                    conv_taps(l, (n - 13) * 31 // 9, (n - 12) * 31 // 9)
                if n == 14:
                    after(l, b_kv=1, b_vb=1)
                    for c in range(2):
                        dve.tensor_tensor(state[:, c::2, :], ub[2 + c][:, :].rearrange("p (g v) -> p g v", g=2),
                                          const("hv", H * DV).unsqueeze(1).to_broadcast([P, 2, H * DV]), ALU.mult).then_inc(*sig("b_kvm"))
                    after(l, b_kvm=2)
                    for c in range(1, 4):
                        if c > 1:
                            after(l, b_S=c - 1)
                        dve.scalar_tensor_tensor(state[:, c, :], state[:, c - 1, :], eb[:, (c + 1) * CH - 1:(c + 1) * CH], state[:, c, :],
                                                 ALU.mult, ALU.add).then_inc(*sig("b_S"))
                    dve.tensor_tensor(st_tmp[:, :, :], mb[2][:, :].rearrange("p (b v) -> p b v", v=DV),
                                      proj[:, BK, TP:NT].unsqueeze(2).to_broadcast([P, TD, DV]), ALU.mult).then_inc(*sig("b_kvd"))
                if n == 15:
                    after(l, b_sd=1)
                    dve.tensor_tensor(st_tmp[:, :, :], st[:, :, :], proj[:, BQ, TP:NT].unsqueeze(2).to_broadcast([P, TD, DV]), ALU.mult)\
                       .then_inc(*sig("b_prod"))
                if n == 16:
                    after(l, past=PAST, lfn_in=16)
                    dve.tensor_tensor_scan(tail[:, :], const("ones", TP, H * TD), lfp[:, :], 0.0, ALU.mult, ALU.add).then_inc(*sig("d_ct"))
                    after(l, d_ct=1)
                    dve.tensor_tensor(dstat[:, 0:1], tail[:, TP - 1:TP], lfn[:, :], ALU.add).then_inc(*sig("d_ct"))
                    after(l, d_ct=2)
                    dve.tensor_scalar(tail[:, :], tail[:, :], -1.0, dstat[:, 0:1], ALU.mult, ALU.add).then_inc(*sig("d_ct"))
                if n == 17:
                    after(l, a_dp=2)
                    dve.tensor_reduce(ymix[:, YA:YA + 2, TP:NT], a_prod[:, :, :, :], AX.X, ALU.add).then_inc(*sig("a_dr"))
                    after(l, a_dr=1)
                    dve.tensor_tensor(ymix[:, YA:YA + 2, TP:NT], ymix[:, YA:YA + 2, TP:NT],
                                      par[:, PAR["acb"]:PAR["acb"] + 2].unsqueeze(2).to_broadcast([P, 2, TD]), ALU.add).then_inc(*sig("a_db"))
                    for h in (0, 1):
                        biased(l, h)
                if n == 18:
                    for h in (2, 3):
                        biased(l, h)
                if n == 19:
                    after(l, d_sm=4)
                    dve.tensor_reduce(stats[:, 0, 0:H], sm[:, :, 0:P], AX.X, ALU.max, negate=True).then_inc(*sig("d_mx"))
                    dve.tensor_reduce(stats[:, 0, H:2 * H], sm[:, :, P:3 * P], AX.X, ALU.max, negate=True).then_inc(*sig("d_mx"))
                    after(l, d_dT=1, d_ct=3)
                    dve.scalar_tensor_tensor(sd[:, 0:TP], mb[3][0:H * TD, 64:64 + TP], DV ** -0.5, tail[:, :], ALU.mult, ALU.add).then_inc(*sig("d_ds"))
                    dve.tensor_scalar(sd[:, TP:TP + 1], mb[3][0:H * TD, 320:321], DV ** -0.5, None, ALU.mult).then_inc(*sig("d_ds"))
                    after(l, d_ds=2)
                    dve.tensor_reduce(dstat[:, 1:2], sd[:, :], AX.X, ALU.max, negate=True).then_inc(*sig("d_dmx"))
                if n == 20:
                    after(l, d_dex=1)
                    dve.reciprocal(dstat[:, 3:4], dstat[:, 2:3]).then_inc(*sig("d_dri"))
                    after(l, d_dri=1)
                    dve.tensor_scalar(sd[:, :], sd[:, :], dstat[:, 3:4], None, ALU.mult).then_inc(*sig("d_dp"))
                    after(l, d_dp=1)
                    dve.tensor_scalar(p_new[:, :], const("dec", TD, H * TD), sd[:, TP:TP + 1], None, ALU.mult).then_inc(*sig("d_dp"))
                    after(l, b_rs=4, b_gs=1)
                    for j in range(2):
                        dve.scalar_tensor_tensor(o_rs[:, j, :], sg[:, j, :], par[:, PAR["bng"] + j:PAR["bng"] + j + 1], o_rs[:, j, :],
                                                 ALU.mult, ALU.mult).then_inc(*sig("b_t"))
                    after(l, b_t=2)
                    dve.tensor_tensor(ymix[:, YB:YB + 2, :], ymix[:, YB:YB + 2, :], o_rs[:, :, :], ALU.mult).then_inc(*sig("b_y"))
                    after(l, d_ex=8)
                    dve.reciprocal(stats[:, 2, :], stats[:, 1, :]).then_inc(*sig("d_ri"))
                    after(l, d_ri=1)
                    for b, part in ((0, slice(0, P)), (1, slice(P, 3 * P))):
                        dve.tensor_tensor(sm[:, :, part], sm[:, :, part],
                                          stats[:, 2, b * H:(b + 1) * H].unsqueeze(2).to_broadcast([P, H, P * (b + 1)]), ALU.mult).then_inc(*sig("d_pn"))
                if n == 22:
                    after(l, a_sum=1)
                    for c in range(2):
                        dve.scalar_tensor_tensor(ymix[:, YA + c, :], ub[2][:, 0:NT], -1.0 / 256, ymix[:, YA + c, :], ALU.mult, ALU.add)\
                           .then_inc(*sig("a_cen"))
                if n == 24:
                    after(l, a_rsd=2)
                    dve.tensor_tensor(ymix[:, YA:YA + 2, :], ymix[:, YA:YA + 2, :], a_rs[:, :].unsqueeze(1).to_broadcast([P, 2, NT]), ALU.mult)\
                       .then_inc(*sig("a_nrm"))
                    after(l, d_dpv=2, proj=18)
                    dve.tensor_tensor(d_tmp[:, :].rearrange("p (j b) -> p j b", j=2), mb[3][:, 480:496].rearrange("p (j b) -> p j b", j=2),
                                      proj[:, DVV:DVV + 2, TP:NT], ALU.mult).then_inc(*sig("d_dt"))
                    after(l, d_dt=1)
                    for i in range(2):
                        r = slice(CH * i, CH * (i + 1))
                        dve.tensor_tensor(ymix[r, YD:YD + 2, TP:NT], mb[3][r, 448 + i:480:2].rearrange("p (j b) -> p j b", j=2),
                                          d_tmp[r, :].rearrange("p (j b) -> p j b", j=2), ALU.add).then_inc(*sig("d_dy"))

            def biased(l, h):
                after(l, d_sc=h + 1)
                dve.scalar_tensor_tensor(sm[:, h, :], mb[h % 2][:, 0:3 * P], DV ** -0.5, const("tri", 3 * P), ALU.mult, ALU.add).then_inc(*sig("d_sm"))

            def mixer(l):
                def evacuate(n):
                    m = IN_WIDTH[n]
                    dve.wait_ge(S["unit_done"], l * UNITS + PHASES["in"][0] + n + 1 + RING)
                    dve.tensor_tensor(proj[0:m, n, :], unit_bank(n)[0:m, 0:NT], rs_h[0:m, :], ALU.mult).then_inc(*sig("proj"))

                def inp(i, s, reps, lead):
                    rest_unit(dve, lead, reps)
                    if s == 1:
                        dve.wait_ge(*at(l, "rh_ready", 4))
                    if s >= 1:
                        evacuate(s - 1)
                    mix(l, s)
                steps(dve, "in", l, inp, 24)
                evacuate(23)
                mix(l, 24)
                for k in range(KD):
                    dve.wait_ge(*at(l, "ym_hi", k + 1))
                    dve.tensor_tensor(ym_lo[:, k, :], ymix[:, k, :], ym_hi[:, k, :].bitcast(F32), ALU.subtract)\
                       .then_inc(*sig("ym_ready"))
                steps(dve, "out", l, lambda i, s, reps, lead: rest_unit(dve, lead, reps), 8)
                boundary(l, 1)

            dve.memset(biases[:, 0:1], EPS).then_inc(started, 1)
            dve.memset(biases[:, 1:2], LN_HALF).then_inc(started, 1)
            dve.memset(biases[:, 2:3], 1.0).then_inc(started, 1)
            for k in range(KD):
                if k < LEAD:
                    rest_unit(dve, first_unit(k), 0)
                dve.wait_ge(S["hg_hi"], k + 1)
                dve.wait_ge(x_in[k], 16 * (1 + (k == 0)))
                dve.scalar_tensor_tensor(hg_lo[:, k, :], resid[:, k, :], gain0[:, k:k + 1], hg_hi[:, k, :].bitcast(F32),
                                         ALU.mult, ALU.subtract).then_inc(S["hg_ready"], 1)
            dve.wait_ge(setup, 16 * 3)
            with dve.Fori(0, L) as l:
                dve.wait_ge(*at(l, "hg_ready", 0))
                dve.tensor_copy(par[:, :], par_all[:, bass.ds(l, 1), :].rearrange("p a c -> p (a c)")).then_inc(*sig("par_ready"))
                feed_forward(l, 0)
                mixer(l)
                feed_forward(l, 2)

        @block.gpsimd
        def _(pool):
            def output_squares(l, q, phase):
                pool.wait_ge(*at(l, "y_sum", q))
                pool.tensor_tensor(y_acc[:, :], con[:, 0:NT], con[:, 0:NT], ALU.subtract).then_inc(*sig("y_acc"))
                for n in range(KD - 1):
                    pool.wait_ge(*at(l, "y_sq", 8 * q + n + 1))
                    pool.wait_ge(*at(l, "y_acc", 8 * q + n + 1))
                    pool.tensor_tensor(y_acc[:, :], y_acc[:, :], y_sq[:, n % 2, :], ALU.add).then_inc(*sig("y_acc"))

            def input_squares(l, q):
                pool.wait_ge(*at(l, "h_sum", q + 1))
                pool.tensor_tensor(h_acc[:, :], con[:, 0:NT], con[:, 0:NT], ALU.subtract).then_inc(*sig("h_acc"))
                for k in range(KD):
                    pool.wait_ge(*at(l, "h_sq", 8 * q + k + 1))
                    pool.wait_ge(*at(l, "h_acc", 9 * q + k + 1))
                    pool.tensor_tensor(h_acc[:, :], h_acc[:, :], h_sq[:, k % 2, :], ALU.add).then_inc(*sig("h_acc"))

            def feed_forward(l, q):
                f = q // 2
                def product(j, b, reps):
                    pool.wait_ge(*at(l, "gu_read", f * 44 + 2 * j + 2))
                    pool.wait_ge(*at(l, "silu_ready", f * 22 + j + 1))
                    pool.wait_ge(*at(l, "act_lo", f * 22 + j - 1))
                    pool.tensor_tensor(act_s[:, b, :], silu_s[:, b, :], up_s[:, b, :], ALU.mult).then_inc(*sig("act_ready", reps))

                def rest(j, b, reps):
                    pool.wait_ge(*at(l, "act_hi", f * 22 + j + 1))
                    pool.tensor_tensor(tile_of(act_lo, j), act_s[:, b, :], tile_of(act_hi, j).bitcast(F32), ALU.subtract)\
                        .then_inc(*sig("act_lo", reps))
                product(0, 0, 1)
                with pool.Fori(0, 10) as i:
                    for b in range(2):
                        product(2 * i + b + 1, 1 - b, 10)
                        rest(2 * i + b, b, 10)
                product(21, 1, 1)
                rest(20, 0, 1)
                rest(21, 1, 1)
                output_squares(l, q, f"dn{f}")
                input_squares(l, q)

            def after(l, **counts):
                for name, k in counts.items():
                    pool.wait_ge(*at(l, name, k))

            def mix(l, n):
                if n == 0:
                    pool.wait_ge(setup, 16 * 3)
                    pool.wait_ge(S["unit_done"], l * UNITS + PHASES["in"][0] + RING)
                    after(l, stored=0)
                    zero = con[:, 0:2 * (TAPS_A - 1)].rearrange("p (a b) -> p a b", a=2)
                    pool.tensor_tensor(a_pad[:, :, 0:TAPS_A - 1], zero, zero, ALU.subtract).then_inc(*sig("a_z"))
                    zero = con[:, 0:H * NT].rearrange("p (a b) -> p a b", a=H)
                    pool.tensor_tensor(qm[:, :, :], zero, zero, ALU.subtract).then_inc(*sig("d_qz"))
                if n == 4:
                    after(l, b_qs=1)
                    pool.tensor_tensor(q_heads[:, :, :], proj[:, BQ, 0:TP].unsqueeze(1).to_broadcast([P, H, TP]),
                                       const("hv", H * DV)[:, ::DV].unsqueeze(2).to_broadcast([P, H, TP]), ALU.mult).then_inc(*sig("b_qb0"))
                    after(l, b_eb=1, b_qb0=1)
                    pool.tensor_tensor(proj[:, BQ, 0:TP], proj[:, BQ, 0:TP], eb[:, 0:TP], ALU.mult).then_inc(*sig("b_qe"))
                if 5 <= n <= 10:
                    i = n - 4
                    after(l, b_E=i)
                    if i >= 2:
                        after(l, b_sc=i)
                    pool.tensor_tensor(q_lv[:, :, :], q_heads[:, :, :], lv[:, 2 + i % 2, :].unsqueeze(1).to_broadcast([P, H, TP]), ALU.mult)\
                        .then_inc(*sig("b_qbl"))
                if n == 11:
                    after(l, a_sg=1, past=PAST)
                    pool.tensor_tensor(a_pad[:, :, TAPS_A - 1:], proj[:, AV:AV + 2, 0:TP], proj[:, AG:AG + 2, 0:TP], ALU.mult).then_inc(*sig("a_in"))
                    pool.tensor_tensor(a_dec[:, :, :, TAPS_A - 1], proj[:, AV:AV + 2, TP:NT], proj[:, AG:AG + 2, TP:NT], ALU.mult)\
                        .then_inc(*sig("a_in"))
                    after(l, proj=12)
                    for j in range(2):
                        pool.tensor_tensor(v_diag[:, j * TD:(j + 1) * TD, :], proj[:, BV + j, TP:NT].unsqueeze(2).to_broadcast([P, TD, DV]),
                                           const("lvm", CH).unsqueeze(1).to_broadcast([P, TD, CH]), ALU.mult).then_inc(*sig("b_vx"))
                    pool.tensor_tensor(st[:, :, :], st[:, :, :], eb[:, TP:NT].unsqueeze(2).to_broadcast([P, TD, DV]), ALU.mult).then_inc(*sig("b_sde"))
                    after(l, b_sg=1)
                    pool.tensor_tensor(sg[:, :, :], sg[:, :, :], proj[:, BG:BG + 2, :], ALU.mult).then_inc(*sig("b_gs"))
                if n == 14:
                    after(l, b_kvd=1, b_sde=1)
                    pool.tensor_tensor(st[:, :, :], st[:, :, :], st_tmp[:, :, :], ALU.add).then_inc(*sig("b_sd"))
                    after(l, a_in=2)
                    for c in range(2):
                        pool.tensor_tensor(a_prod[:, c, :, :], a_dec[:, c, :, :],
                                           par[:, PAR["acw"] + c * TAPS_A:PAR["acw"] + (c + 1) * TAPS_A].unsqueeze(1).to_broadcast([P, TD, TAPS_A]),
                                           ALU.mult).then_inc(*sig("a_dp"))
                if n == 16:
                    after(l, d_qm=2, proj=16)
                    for j in range(2):
                        pool.tensor_tensor(pm[:, 2 * j:2 * j + 2, :], qm[:, 2 * j:2 * j + 2, TP:NT],
                                           proj[:, DKK + j, TP:NT].unsqueeze(1).to_broadcast([P, 2, TD]), ALU.mult).then_inc(*sig("d_pm"))
                if n == 24:
                    short_conv(l)

            def short_conv(l):
                after(l, proj=24, b_y=1)
                pool.tensor_tensor(z_pad[:, :, 0:2], con[:, 0:4].rearrange("p (a b) -> p a b", a=2), con[:, 0:4].rearrange("p (a b) -> p a b", a=2),
                                   ALU.subtract).then_inc(*sig("c_z"))
                pool.tensor_tensor(z_pad[:, :, 2:], proj[:, CC:CC + 2, 0:TP], proj[:, CX:CX + 2, 0:TP], ALU.mult).then_inc(*sig("c_z"))
                pool.tensor_tensor(z_dec[:, :, :, 2], proj[:, CC:CC + 2, TP:NT], proj[:, CX:CX + 2, TP:NT], ALU.mult).then_inc(*sig("c_z"))
                after(l, c_z=3)
                done = 0
                for t in range(TAPS_C):
                    out = c_tmp if t else ymix[:, YC:YC + 2, :]
                    w = par[:, PAR["ccw"] + t:PAR["ccw"] + 6:TAPS_C].unsqueeze(2)
                    pool.tensor_tensor(out[:, :, 0:TP], z_pad[:, :, t:t + TP], w.to_broadcast([P, 2, TP]), ALU.mult).then_inc(*sig("c_t"))
                    pool.tensor_tensor(out[:, :, TP:NT], z_dec[:, :, :, t], w.to_broadcast([P, 2, TD]), ALU.mult).then_inc(*sig("c_t"))
                    done += 2
                    if t:
                        after(l, c_t=done)
                        pool.tensor_tensor(ymix[:, YC:YC + 2, :], ymix[:, YC:YC + 2, :], c_tmp, ALU.add).then_inc(*sig("c_t"))
                        done += 1
                        after(l, c_t=done)
                pool.tensor_tensor(ymix[:, YC:YC + 2, :], ymix[:, YC:YC + 2, :], proj[:, CB:CB + 2, :], ALU.mult).then_inc(*sig("c_y"))

            for n, name in enumerate(("split_done", "unit_done", "gu_read", "y_scaled", "silu_ready", "act_ready", "act_lo", "y_acc", "y_sum", "stored")):
                pool.memset(z_t[:, 0, n:n + 1], 0.0).then_inc(S[name], INIT[name])
            pool.memset(h_acc[:, :], 0.0).then_inc(S["h_acc"], 1)
            for k in range(KD):
                pool.wait_ge(S["h_sq"], k + 1)
                pool.wait_ge(S["h_acc"], k + 1)
                pool.tensor_tensor(h_acc[:, :], h_acc[:, :], h_sq[:, k % 2, :], ALU.add).then_inc(S["h_acc"], 1)
            with pool.Fori(0, L) as l:
                feed_forward(l, 0)
                for n in (0, 4, 5, 6, 7, 8, 9, 10, 11, 14, 16, 24):
                    mix(l, n)
                output_squares(l, 1, "out")
                input_squares(l, 1)
                feed_forward(l, 2)
OUTS = {"h": (P, KD, NT), "kv": (L, P, 4 * NT), "pf": (L, H, TP), "sf": (L, H * TD, 1), "sb": (L, P, TD * DV), "pc": (L, P, 2, 2)}
for _c in range(2):
    OUTS[f"pa{_c}"] = (L, P, TAPS_A - 1)
    OUTS[f"sa{_c}"] = (L, P, TD, TAPS_A - 1)
    OUTS[f"sc{_c}"] = (L, P, TD, 2)
for _h in range(H):
    OUTS[f"pb{_h}"] = (L, DK, DV)


def states_in(a, g):
    import numpy as np
    f = np.ascontiguousarray
    for c in range(2):
        part = slice(c * P, (c + 1) * P)
        a[f"state_a{c}"] = f(g["state_conv_a"][..., part].transpose(0, 3, 1, 2))
        a[f"state_c{c}"] = f(g["state_conv_c"][..., part].transpose(0, 3, 1, 2))
    a["state_b"] = f(g["state_gla"].transpose(0, 2, 3, 1, 4)).reshape(L, P, TD * DV)
    a["cache_k"] = f(g["cache_k"].reshape(L * NPOOL, PAGE, 2, P).transpose(0, 3, 2, 1)).reshape(L * NPOOL, P, 2 * PAGE)
    a["cache_v"] = f(g["cache_v"]).reshape(L * NPOOL, PAGE, H * DV)
    a["cache_f"] = f(g["cache_logf"].transpose(0, 1, 3, 2)).reshape(L * NPOOL, H, PAGE)
    a["table"] = f(g["page_table"]).reshape(1, TD * NPAGES)


def results(r):
    import numpy as np
    h = r["h"].transpose(2, 1, 0).reshape(NT, D)
    kv = r["kv"].reshape(L, P, 2, 2, NT).transpose(2, 0, 4, 3, 1).reshape(2, L, NT, H, DV)
    two = lambda n: np.stack([r[n + "0"], r[n + "1"]], 1)
    pa = two("pa").transpose(0, 3, 1, 2).reshape(L, 1, TAPS_A - 1, 2 * P)
    sa = two("sa").transpose(0, 3, 4, 1, 2).reshape(L, TD, TAPS_A - 1, 2 * P)
    pb = np.stack([r[f"pb{i}"] for i in range(H)], 1).reshape(L, 1, H, DK, DV)
    sb = r["sb"].reshape(L, H, DK, TD, DV).transpose(0, 3, 1, 2, 4)
    pc = r["pc"].transpose(0, 3, 2, 1).reshape(L, 1, 2, 2 * P)
    sc = two("sc").transpose(0, 3, 4, 1, 2).reshape(L, TD, 2, 2 * P)
    pf = r["pf"].transpose(0, 2, 1).reshape(L, 1, TP, H)
    sf = r["sf"].reshape(L, H, TD).transpose(0, 2, 1).reshape(L, TD, 1, H)
    return (h[None, :TP], h[TP:, None], pa, pb, pc, kv[0, :, None, :TP], kv[1, :, None, :TP], pf,
            sa, sb, sc, kv[0, :, TP:, None], kv[1, :, TP:, None], sf)


def build(nc, ins, outs):
    tally = {}
    decoder_kernel(nc, ins, outs, PERS, tally)
    assert tally == PERS, {k: (PERS.get(k), tally.get(k)) for k in set(PERS) | set(tally) if PERS.get(k) != tally.get(k)}


PERS = {
    "past": 336, "pages_in": 512, "stored": 240, "lfn_in": 16, "unit_done": 168, "h_sum": 3, "y_sum": 3, "b_z":
    1, "b_sc": 7, "b_vT": 1, "b_kdT": 1, "b_vb": 1, "b_kv": 1, "d_dsc": 2, "b_o": 1, "b_od": 1, "d_sc": 4,
    "b_gn": 1, "d_dT": 1, "d_vT": 1, "d_dpT": 1, "d_pT": 4, "d_dpv": 2, "a_sum": 1, "d_o": 1, "a_var": 1,
    "hi_ready": 168, "rh_ready": 6, "silu_ready": 44, "act_hi": 44, "y_sq": 24, "y_scaled": 24, "ry_ready": 6,
    "hg_hi": 24, "h_sq": 24, "b_sp": 3, "d_sp": 3, "b_qs": 1, "b_eb": 1, "b_E": 7, "a_sg": 1, "b_sg": 1, "b_vt":
    1, "b_kdt": 1, "d_qm": 2, "b_og": 3, "b_osq": 1, "d_scs": 1, "b_rs": 4, "d_vt": 1, "d_dex": 1, "d_ex": 8,
    "d_ptd": 1, "d_pt": 4, "a_sq": 1, "a_rsd": 2, "d_y": 1, "a_y": 2, "ym_hi": 8, "split_done": 168,
    "par_ready": 1, "gu_read": 88, "z_ready": 24, "h_ready": 24, "hg_ready": 24, "proj": 24, "b_la": 2, "b_bc":
    2, "d_lf": 2, "b_D": 13, "d_cf": 2, "b_kt": 7, "b_msk": 7, "b_asc": 6, "a_tap": 62, "b_kvm": 2, "b_S": 3,
    "b_kvd": 1, "b_prod": 1, "d_ct": 3, "a_dr": 1, "a_db": 1, "d_sm": 4, "d_mx": 2, "d_ds": 2, "d_dmx": 1,
    "d_dri": 1, "d_dp": 2, "b_t": 2, "b_y": 1, "d_ri": 1, "d_pn": 2, "a_cen": 2, "a_nrm": 1, "d_dt": 1, "d_dy":
    2, "ym_ready": 8, "act_ready": 44, "act_lo": 44, "y_acc": 24, "h_acc": 27, "a_z": 1, "d_qz": 1, "b_qb0": 1,
    "b_qe": 1, "b_qbl": 6, "a_in": 2, "b_vx": 2, "b_sde": 1, "b_gs": 1, "b_sd": 1, "a_dp": 2, "d_pm": 2, "c_z":
    3, "c_t": 8, "c_y": 1
}


def packed(a, k, n):
    import numpy as np
    return np.ascontiguousarray(a.reshape(L, k, P, n, P).transpose(0, 3, 2, 1, 4)).reshape(L * n, P, k * P)


def kernel(**inputs):
    import numpy as np
    import concourse.bacc as _bacc
    from concourse.bass_utils import run_bass_kernel_spmd as _run

    g = {k: np.asarray(v) for k, v in inputs.items()}
    f32 = np.float32
    a = {}

    for f in (0, 1):
        gate, up = (packed(g[f"ffn{f + 1}_w_{n}"], KD, KF) for n in ("gate", "up"))
        gu = np.stack([gate, up], 1).reshape(L * 44, P, COLS)
        a[f"w_gu{f}"] = np.concatenate([gu, np.zeros((LEAD, P, COLS), f32)])
        dn = packed(g[f"ffn{f + 1}_w_down"], KF, KD)
        dn = np.concatenate([dn, np.zeros((L * KD, P, 2 * P), f32)], 2)
        a[f"w_dn{f}"] = np.ascontiguousarray(dn.reshape(L * KD, P, 3, COLS).transpose(0, 2, 1, 3)).reshape(L * 24, P, COLS)
    order = {YA: 0, YB: 2, YC: 4, YD: 6}
    rows = [order[t - t % 2] + t % 2 for t in range(KD)]
    a["w_out"] = packed(g["w_out"].reshape(L, KD, P, D)[:, rows].reshape(L, D, D), KD, KD)
    w = g["w_in"]
    off_b, off_c, off_d = 512, 512 + 784, 512 + 784 + 768
    at = {ALR: off_b + 768, FG: off_d + 768, BQ: off_b, BK: off_b + 128, AV: 0, AV + 1: 128, AG: 256, AG + 1: 384,
          BG: off_b + 512, BG + 1: off_b + 640, BV: off_b + 256, BV + 1: off_b + 384}
    for i in range(6):
        at[DQ + i] = off_d + i * P
        at[CB + i] = off_c + i * P
    win = np.zeros((L, 24, P, COLS), f32)
    for n in range(24):
        m = IN_WIDTH[n]
        win[:, n, :, 0:KD * m] = w[:, :, at[n]:at[n] + m].reshape(L, KD, P, m).transpose(0, 2, 1, 3).reshape(L, P, KD * m)
    a["w_in"] = win.reshape(L * 24, P, COLS)

    def tiles(x):
        return x.reshape(L, -1, P).transpose(2, 0, 1)

    par = np.zeros((P, L, NPAR), f32)

    def put(name, x, off=0):
        par[0:x.shape[0], :, PAR[name] + off:PAR[name] + off + x.shape[2]] = x
    put("pre", tiles(g["mix_pre_g"]), 0)
    put("pre", tiles(g["ffn2_pre_g"]), 8)
    put("pre", np.roll(tiles(g["ffn1_pre_g"]), -1, 1), 16)
    put("post", tiles(g["ffn1_post_g"]), 0)
    put("post", tiles(g["mix_post_g"]), 8)
    put("post", tiles(g["ffn2_post_g"]), 16)
    put("acw", g["a_conv_w"].reshape(L, TAPS_A, 2, P).transpose(3, 0, 2, 1).reshape(P, L, 62))
    put("acb", tiles(g["a_conv_b"]))
    put("alg", tiles(g["a_ln_g"]))
    put("alb", tiles(g["a_ln_b"]))
    put("ba", tiles(g["b_gate_b"]))
    put("bng", tiles(g["b_out_norm_g"]))
    put("ccw", g["c_conv_w"].reshape(L, TAPS_C, 2, P).transpose(3, 0, 2, 1).reshape(P, L, 6))
    put("bf", g["d_forget_b"].T.reshape(H, L, 1))
    put("wa2", g["b_gate_w2"].transpose(1, 0, 2))
    a["par"] = par
    a["gain0"] = np.ascontiguousarray(tiles(g["ffn1_pre_g"])[:, 0])

    con = np.zeros((P, NCON), f32)

    def const(name, x):
        con[0:x.shape[0], CON[name]:CON[name] + x.shape[1]] = x
    p = np.arange(P)
    const("ident", np.eye(P, dtype=f32))
    const("ones", np.ones((P, TP), f32))
    const("blk", (p[:, None] // DV == p[None, :] // DV).astype(f32))
    tri = np.where(p[None, :] <= p[:, None], 0.0, -1e30).astype(f32)
    const("tri", np.concatenate([tri, np.zeros((P, P), f32), tri], 1))
    s, t = p[:, None] % CH, np.arange(CH)[None, :]
    masks = [(s == t) if m == 0 else (s // (2 * m) == t // (2 * m)) & (s % (2 * m) < m) & (t % (2 * m) >= m) for m in LEVELS]
    const("lvm", np.concatenate(masks, 1).astype(f32))
    const("rst", np.broadcast_to((np.arange(TP) % CH != 0).astype(f32), (P, TP)))
    const("hv", (p[:, None] // DK == np.arange(H * DV)[None, :] // DV).astype(f32))
    const("sel", (np.arange(H)[:, None] == np.arange(H * P)[None, :] // P).astype(f32))
    const("hvt", np.concatenate([2 * j + p[:, None] // DV == p[None, :] // DK for j in range(2)], 1).astype(f32))
    r = np.arange(H * TD)[:, None]
    const("heads", (r // TD == np.arange(2 * P)[None, :] // DV).astype(f32))
    const("dec", (r % TD == np.arange(TD)[None, :]).astype(f32))
    a["con"] = con

    x = np.concatenate([g["x_prompt"].reshape(TP, D), g["x_sample"].reshape(TD, D)])
    a["x"] = np.ascontiguousarray(x.T.reshape(KD, P, NT).transpose(1, 0, 2))
    states_in(a, g)

    nc = _bacc.Bacc("TRN2", target_bir_lowering=False, num_devices=1)
    ins = {n: nc.dram_tensor("in_" + n, v.shape, mybir.dt.from_np(v.dtype), kind="ExternalInput").ap() for n, v in a.items()}
    outs = {n: nc.dram_tensor("out_" + n, s, F32, kind="ExternalOutput").ap() for n, s in OUTS.items()}
    build(nc, ins, outs)
    r = _run(nc, [{"in_" + n: v for n, v in a.items()}], core_ids=[0]).results[0]
    return results({n: np.asarray(r["out_" + n]) for n in OUTS})
```

```python
from contextlib import ExitStack

import concourse.bass as bass
from concourse import mybir

F32 = mybir.dt.float32
F32R = mybir.dt.float32r
I32 = mybir.dt.int32
ALU = mybir.AluOpType
ACT = mybir.ActivationFunctionType
AX = mybir.AxisListType

P = 128
L = 2
D = 1024
TP, TD = 256, 8
NT = TP + TD
KD = D // P
FF = 2816
KF = FF // P
NPOOL, PAGE, NPAGES = 20, 128, 2
EPS = 1e-6
LN_HALF = -0.6931471805599453
TAPS_A, TAPS_C = 31, 3
H = 4
DK, DV, CH = 32, 64, 64
GLA_TAU = 16.0
COLS = KD * P

ALR, FG, BQ, BK, AV, AG, BG, BV, DQ, DKK, DVV, CB, CC, CX = 0, 1, 2, 3, 4, 6, 8, 10, 12, 14, 16, 18, 19, 20
IN_WIDTH = [16, 4] + [P] * 22

RING = 4
PHASES = {"gu0": (0, 44), "dn0": (44, 24), "in": (68, 24), "out": (92, 8), "gu1": (100, 44), "dn1": (144, 24)}
ORDER = list(PHASES)
UNITS = 168
GROUP = 3
LEAD = 3
DN_TILES = [8, 8, 6]

PAR = {}
_at = 0
for _n, _w in (("pre", 24), ("post", 24), ("acw", 62), ("acb", 2), ("alg", 2), ("alb", 2), ("ba", 1),
               ("bng", 2), ("ccw", 6), ("bf", 1), ("wa2", P)):
    PAR[_n] = _at
    _at += _w
NPAR = _at

CON = {}
_at = 0
for _n, _w in (("ident", 128), ("ones", TP), ("blk", 128), ("tri", 3 * P), ("lvm", 7 * CH), ("rst", TP),
               ("hv", H * DV), ("hvt", 2 * P), ("sel", H * P), ("heads", 2 * P), ("dec", TD)):
    CON[_n] = _at
    _at += _w
NCON = _at
LEVELS = [0, 32, 16, 8, 4, 2, 1]

YB, YC, YD, YA = 0, 2, 4, 6

PATTERN = {"gu0": 4, "dn0": 12, "in": 24, "out": 8, "gu1": 4, "dn1": 12}
PAST = 16 * (5 + TD * NPAGES)
A_DVE = 20
STORE = 4
WARM = 8
TAPS = {n: ((n - 12) * A_DVE // 8, (n - 11) * A_DVE // 8) for n in range(12, 20)}
INIT = {"split_done": RING, "unit_done": RING, "gu_read": 4, "y_scaled": 2, "silu_ready": 2, "act_ready": 2, "act_lo": 2,
        "hg_hi": 8, "h_sq": 8, "h_acc": 9, "hg_ready": 8, "y_acc": 1, "y_sum": 1, "stored": 1}


def decoder_kernel(nc, ins, outs, per, tally):
    with ExitStack() as ctx:
        def sb(name, shape, dt=F32, scope=ctx):
            return scope.enter_context(nc.sbuf_tensor(name, shape, dt))

        resid = sb("resid", [P, KD, NT])
        hg_hi = sb("hg_hi", [P, KD, NT], F32R)
        hg_lo = sb("hg_lo", [P, KD, NT], F32R)
        yg = sb("yg", [P, KD, NT])
        ymix = yg
        raw = sb("raw", [P, RING, COLS])
        w_hi = sb("w_hi", [P, RING, COLS], F32R)
        w_lo = sb("w_lo", [P, RING, COLS], F32R)
        par_all = sb("par_all", [P, L, NPAR])
        par = sb("par", [P, NPAR])
        gain0 = sb("gain0", [P, KD])
        con = sb("con", [P, NCON])
        biases = sb("biases", [P, 3])
        rs_y = sb("rs_y", [P, NT])
        rs_h = sb("rs_h", [P, NT])
        ln_t = sb("ln_t", [P, NT])
        y_acc = sb("y_acc", [P, NT])
        h_acc = sb("h_acc", [P, NT])
        y_sq = sb("y_sq", [P, 2, NT])
        h_sq = sb("h_sq", [P, 2, NT])
        z_t = sb("z_t", [P, 2, NT])
        with ExitStack() as scope:
            act_hi = sb("act_hi", [P, KF, NT], F32R, scope)
            act_lo = sb("act_lo", [P, KF, NT], F32R, scope)
            gate_s = sb("gate_s", [P, 2, NT], F32, scope)
            up_s = sb("up_s", [P, 2, NT], F32, scope)
            silu_s = sb("silu_s", [P, 2, NT], F32, scope)
            act_s = sb("act_s", [P, 2, NT], F32, scope)
        proj = sb("proj", [P, 24, NT])
        ym_hi = sb("ym_hi", [P, KD, NT], F32R)
        ym_lo = sb("ym_lo", [P, KD, NT], F32R)
        lv = sb("lv", [P, 6, TP])
        lvf = lv[:, :, :].rearrange("p a b -> p (a b)")
        o_sq = lvf[:, 0:2 * NT].rearrange("p (a b) -> p a b", a=2)
        o_rs = lvf[:, 2 * NT:4 * NT].rearrange("p (a b) -> p a b", a=2)
        c_tmp = lvf[:, 0:NT]
        with ExitStack() as scope:
            q_heads = sb("q_heads", [P, H, TP], F32, scope)
            q_lv = sb("q_lv", [P, H, TP], F32, scope)
            scores = sb("scores", [P, 512], F32, scope)
            level = sb("level", [P, 512], F32, scope)
        sm = sb("sm", [P, H, 3 * P])
        smT = sb("smT", [P, H, 3 * P])
        smT_flat = smT[:, :, :].rearrange("p a b -> p (a b)")
        a_prod = smT_flat[:, 0:2 * TD * TAPS_A].rearrange("p (c b t) -> p c b t", c=2, b=TD)
        lft = ln_t[0:H, :]
        vtok = sb("vtok", [P, 2, TP])
        kdt = sb("kdt", [P, 2, P])
        state = sb("state", [P, H, H * DV])
        v_diag = state[:, :, :].rearrange("p a (b v) -> p (a b) v", v=DV)
        st_tmp = sb("st_tmp", [P, TD, DV])
        sg = sb("sg", [P, 2, NT])
        a_pad = sb("a_pad", [P, 2, TAPS_A - 1 + TP])
        qm = sb("qm", [P, H, NT])
        tail = sb("tail", [H * TD, TP])
        sd = sb("sd", [H * TD, TP + 1])
        sct = sb("sct", [P, 64])
        pm = sb("pm", [P, H, TD])
        ptd = sb("ptd", [P, 2, H, TD])
        p_new = sb("p_new", [H * TD, TD])
        stats = sb("stats", [P, 3, 8])
        dstat = sb("dstat", [H * TD, 4])
        d_tmp = sb("d_tmp", [P, 16])
        a_dec = sb("a_dec", [P, 2, TD, TAPS_A])
        z_dec = sb("z_dec", [P, 2, TD, TAPS_C])
        st = sb("st", [P, TD, DV])
        lfp = sb("lfp", [H * TD, TP])
        lfn = sb("lfn", [H * TD, 1])
        pages = sb("pages", [P, 16, TP])
        table = sb("table", [1, TD * NPAGES], I32)
        z_pad = lvf[:, 2 * NT:2 * NT + 2 * (TP + 2)].rearrange("p (a b) -> p a b", a=2)
        a_part, a_term = (y_acc, h_acc), (rs_y, ln_t)
        la, bc = z_t[:, 0, :], z_t[:, 1, :]
        soft, eb = h_sq[:, 0, :], h_sq[:, 1, :]
        a_rs = h_sq[:, 0, :]
        a_sqr = sg
        lf, cf = y_sq[0:H, 0, :], y_sq[0:H, 1, :]

        ub = [ctx.enter_context(nc.psum_tensor(f"ub{i}", [P, 512], F32)) for i in range(4)]
        mb = [ctx.enter_context(nc.psum_tensor(f"mb{i}", [P, 512], F32)) for i in range(4, 8)]
        NORM = mb[3][:, 0:NT]
        fox_bank = (mb[0], mb[1], ub[2], ub[3])

        S = {n: ctx.enter_context(nc.semaphore(n)) for n in per}
        landed = [ctx.enter_context(nc.semaphore(f"landed{i}")) for i in range(RING)]
        x_in = [ctx.enter_context(nc.semaphore(f"x_in{k}")) for k in range(KD)]
        setup = ctx.enter_context(nc.semaphore("setup"))
        started = ctx.enter_context(nc.semaphore("started"))

        def sig(name, times=1, n=1):
            tally[name] = tally.get(name, 0) + n * times
            return S[name], n

        def at(l, name, k):
            assert not isinstance(k, int) or k + INIT.get(name, 0) > 0, (name, k)
            return S[name], l * per[name] + k + INIT.get(name, 0)

        def const(name, cols, part=P):
            return con[0:part, CON[name]:CON[name] + cols]

        ident, ones, blk = const("ident", P), const("ones", P), const("blk", P)

        def tile_of(tiles, n):
            return tiles[:, n, :] if isinstance(n, int) else tiles[:, bass.ds(n, 1), :].rearrange("p a c -> p (a c)")

        def steps(eng, phase, l, body, pattern=4, peel_first=False):
            first, n = PHASES[phase]
            turns = n // pattern

            def turn(i, reps):
                for s in range(pattern):
                    idx, ph, row = i * pattern + s + LEAD, phase, l
                    if reps == 1 and idx >= n:
                        ph, idx = ORDER[(ORDER.index(phase) + 1) % len(ORDER)], idx - n
                        row = l + 1 if phase == "dn1" else l
                    width = DN_TILES[(s + LEAD) % 3] * P if ph.startswith("dn") else COLS
                    if ph.startswith("dn") and ph != phase:
                        width = DN_TILES[idx % 3] * P
                    if ph == "in":
                        width = KD * IN_WIDTH[idx]
                    body(i, s, reps, dict(
                        weights=ins["w_" + ph], row=row * PHASES[ph][1] + idx, width=width,
                        slot=(s + LEAD) % RING, number=l * UNITS + first + i * pattern + s + LEAD,
                        turn=l * (UNITS // RING) + first // RING + i * (pattern // RING) + (s + LEAD) // RING))
            if peel_first:
                turn(0, 1)
            if turns > 1 + peel_first:
                with eng.Fori(int(peel_first), turns - 1) as i:
                    turn(i, turns - 1 - peel_first)
            turn(turns - 1, 1)

        def load_unit(eng, lead, reps):
            row = eng.snap(lead["row"])
            eng.wait_ge(S["split_done"], lead["number"] + 1)
            eng.dma_start(raw[:, lead["slot"], 0:lead["width"]],
                          lead["weights"][bass.ds(row, 1), :, 0:lead["width"]].rearrange("a p c -> p (a c)"))\
               .then_inc(landed[lead["slot"]], 16)

        def round_unit(eng, lead, reps):
            w, slot = lead["width"], lead["slot"]
            eng.wait_ge(landed[slot], (lead["turn"] + 1) * 16)
            eng.wait_ge(S["unit_done"], lead["number"] + 1)
            eng.activation(w_hi[:, slot, 0:w], raw[:, slot, 0:w], ACT.Copy).then_inc(*sig("hi_ready", reps))

        def rest_unit(eng, lead, reps):
            w, slot = lead["width"], lead["slot"]
            eng.wait_ge(S["hi_ready"], lead["number"] + 1)
            eng.tensor_tensor(w_lo[:, slot, 0:w], raw[:, slot, 0:w], w_hi[:, slot, 0:w].bitcast(F32), ALU.subtract)\
               .then_inc(*sig("split_done", reps))

        def first_unit(s):
            return dict(weights=ins["w_gu0"], row=s, width=COLS, slot=s, number=s, turn=0)

        def multiply_unit(eng, out, slot, x_hi, x_lo, tiles, k0, first, last, reps, ready=None):
            for k in range(tiles):
                if ready:
                    ready(k0 + k)
                a_hi, a_lo = (w[:, slot, k * P:(k + 1) * P] for w in (w_hi, w_lo))
                eng.matmul(out, a_hi, x_hi[:, k0 + k, :], start=(first and k == 0), stop=False)
                eng.matmul(out, a_hi, x_lo[:, k0 + k, :], start=False, stop=False)
                mm = eng.matmul(out, a_lo, x_hi[:, k0 + k, :], start=False, stop=(last and k == tiles - 1))
            mm.then_inc(*sig("unit_done", reps))

        def unit_bank(n):
            return ub[n if n < 4 else n % 2]

        def multiply_first(eng, l, phase, x_hi, x_lo, banks, widths, ready, count):
            for k in range(KD):
                for s in range(GROUP):
                    m = widths[s]
                    if k == 0:
                        eng.wait_ge(S["split_done"], l * UNITS + PHASES[phase][0] + s + 1 + RING)
                    if s == 0:
                        eng.wait_ge(*at(l, ready, count + k + 1))
                    a_hi, a_lo = (w[:, s, k * m:(k + 1) * m] for w in (w_hi, w_lo))
                    out = banks[s][0:m, 0:NT]
                    eng.matmul(out, a_hi, x_hi[:, k, :], start=k == 0, stop=False)
                    eng.matmul(out, a_hi, x_lo[:, k, :], start=False, stop=False)
                    mm = eng.matmul(out, a_lo, x_hi[:, k, :], start=False, stop=k == KD - 1)
                    if k == KD - 1:
                        mm.then_inc(*sig("unit_done"))

        block = ctx.enter_context(nc.Block())

        @block.sync
        def _(sp):
            sp.dma_start(gain0[:, :], ins["gain0"]).then_inc(x_in[0], 16)
            for k in range(KD):
                if k < LEAD:
                    sp.dma_start(raw[:, k, :], ins["w_gu0"][k, :, :]).then_inc(landed[k], 16)
                sp.dma_start(resid[:, k, :], ins["x"][:, k, :]).then_inc(x_in[k], 16)
            sp.dma_start(con[:, :], ins["con"]).then_inc(setup, 16)
            sp.dma_start(par_all[:, :, :], ins["par"]).then_inc(setup, 16)
            sp.dma_start(table[:, :], ins["table"]).then_inc(setup, 16)

            sp.wait_ge(setup, 16 * 3)

            def page_row(l, e):
                return sp.snap(l * NPOOL + sp.value_load(table[0:1, e:e + 1], min_val=0, max_val=NPOOL - 1))

            def load_past(l, s):
                def load(dst, src):
                    sp.dma_start(dst, ins[src][bass.ds(l, 1)].rearrange("a p c -> p (a c)")).then_inc(*sig("past", n=16))
                def load3(src, dst):
                    for c in range(2):
                        sp.dma_start(dst[:, c], ins[src + str(c)][bass.ds(l, 1)].rearrange("a p b t -> p (a b) t")).then_inc(*sig("past", n=16))
                if s < TD * NPAGES:
                    b, g = s // NPAGES, s % NPAGES
                    page = page_row(l, s)
                    if s == 0:
                        sp.wait_ge(*at(l, "stored", 0))
                    sp.dma_start(lfp[b:H * TD:TD, g * PAGE:(g + 1) * PAGE],
                                 ins["cache_f"][bass.ds(page, 1)].rearrange("a p c -> p (a c)")).then_inc(*sig("past", n=16))
                    sp.dma_start(pages[:, s, :], ins["cache_k"][bass.ds(page, 1)].rearrange("a p c -> p (a c)"))\
                      .then_inc(*sig("keys_in", n=16))
                if s == 16:
                    load(st[:, :, :].rearrange("p a b -> p (a b)"), "state_b")
                if s == 18:
                    load3("state_a", a_dec[:, :, :, 0:TAPS_A - 1])
                if s == 20:
                    load3("state_c", z_dec[:, :, :, 0:TAPS_C - 1])

            def load_values(l, e):
                page = page_row(l, e)
                if e % 8 == 0:
                    sp.wait_ge(*at(l, "d_dsc", e // 8 + 1))
                sp.dma_start(pages[:, e, :], ins["cache_v"][bass.ds(page, 1)].rearrange("a p c -> p (a c)"))\
                  .then_inc(*sig("values_in0" if e < 8 else "values_in1", n=16))

            def store(l, name, src, **kw):
                dst = outs[name][bass.ds(l, 1)]
                sp.dma_start(dst.rearrange("a p c -> p (a c)"), src, **kw).then_inc(*sig("stored", n=16))

            def store_states(l):
                sp.wait_ge(*at(l, "proj", 18))
                sp.wait_ge(*at(l, "a_in", 2))
                store(l, "kv", proj[:, DKK:DKK + 4, :].rearrange("p a b -> p (a b)"))
                for c in range(2):
                    store(l, f"pa{c}", a_pad[:, c, TP:TP + TAPS_A - 1])
                    sp.dma_start(outs[f"sa{c}"][bass.ds(l, 1)].rearrange("a p b t -> p (a b) t"), a_dec[:, c, :, 1:TAPS_A])\
                      .then_inc(*sig("stored", n=16))
                sp.wait_ge(*at(l, "b_S", 3))
                for h in range(H):
                    store(l, f"pb{h}", state[h * DK:(h + 1) * DK, 3, h * DV:(h + 1) * DV])
                sp.wait_ge(*at(l, "b_sd", 1))
                store(l, "sb", st[:, :, :].rearrange("p a b -> p (a b)"))
                sp.wait_ge(*at(l, "c_z1", 3))
                sp.wait_ge(*at(l, "c_z", 3))
                sp.dma_start(outs["pc"][bass.ds(l, 1)].rearrange("a p c t -> p (a c) t"), z_pad[:, :, TP:TP + 2]).then_inc(*sig("stored", n=16))
                for c in range(2):
                    sp.dma_start(outs[f"sc{c}"][bass.ds(l, 1)].rearrange("a p b t -> p (a b) t"), z_dec[:, c, :, 1:3])\
                      .then_inc(*sig("stored", n=16))

            def mix(l, n):
                if n == 13:
                    sp.wait_ge(*at(l, "d_lf", 2))
                    store(l, "pf", lf[:, 0:TP])
                    sp.dma_start(outs["sf"][bass.ds(l, 1)].rearrange("a (h b) o -> h (a b o)", h=H), lf[:, TP:NT])\
                      .then_inc(*sig("stored", n=16))
                if n == 16:
                    sp.wait_ge(*at(l, "stored", 32))
                    sp.dma_start(lfn[:, :], outs["sf"][bass.ds(l, 1)].rearrange("a p o -> p (a o)"), allow_slow_non_contiguous=True)\
                      .then_inc(*sig("lfn_in", n=16))
                if 18 <= n < 26:
                    for e in (2 * (n - 18), 2 * (n - 18) + 1):
                        load_values(l, e)

            with sp.Fori(0, L) as l:
                for phase in ORDER:
                    def turn(i, s, reps, lead):
                        load_unit(sp, lead, reps)
                        if phase == "dn0":
                            load_past(l, s)
                        if phase == "in":
                            mix(l, s)
                        if phase == "out" and s < 2:
                            mix(l, 24 + s)
                        if phase == "out" and s == STORE:
                            store_states(l)
                    steps(sp, phase, l, turn, 24 if phase == "dn0" else PATTERN[phase])
            sp.wait_ge(S["stored"], L * per["stored"] + INIT["stored"])
            for k in range(KD):
                sp.wait_ge(*at(L - 1, "h_ready", 16 + k + 1))
                sp.dma_start(outs["h"][:, k, :], resid[:, k, :]).then_inc(setup, 16)
            sp.wait_ge(setup, 16 * (3 + KD))

        @block.tensor
        def _(pe):
            def feed_forward(l, q):
                f = q // 2
                gu, dn = f"gu{f}", f"dn{f}"

                def gate_up(i, s, reps):
                    t = i * 4 + s
                    pe.wait_ge(S["split_done"], l * UNITS + PHASES[gu][0] + t + 1 + RING)
                    pe.wait_ge(*at(l, "gu_read", f * 44 + t - 3))
                    multiply_unit(pe, ub[s][:, 0:NT], s, hg_hi, hg_lo, KD, 0, True, True, reps)

                pe.wait_ge(*at(l, "gu_read", f * 44))
                multiply_first(pe, l, gu, hg_hi, hg_lo, ub, [P] * GROUP, "hg_ready", 8 * (q - 1))
                pe.wait_ge(setup, 16 * 3)
                pe.wait_ge(*at(l, "h_acc", 9 * q))
                pe.matmul(NORM, ones, h_acc[:, :], start=True, stop=True).then_inc(*sig("h_sum"))
                gate_up(0, 3, 1)
                with pe.Fori(0, 2) as i:
                    for s in range(20):
                        gate_up(i * 5 + s // 4 + 1, s % 4, 2)
                pe.wait_ge(*at(l, "gu_read", f * 44 + 42))

                def down(i, s, reps):
                    n, part = i * 4 + s // 3, s % 3
                    pe.wait_ge(S["split_done"], l * UNITS + PHASES[dn][0] + i * 12 + s + 1 + RING)
                    if part == 0:
                        pe.wait_ge(*at(l, "y_scaled", q * 8 + n - 1))
                    multiply_unit(pe, ub[s // 3 % 2][:, 0:NT], s % RING, act_hi, act_lo, DN_TILES[part], 8 * part,
                                  part == 0, part == 2, reps,
                                  ready=(lambda k: pe.wait_ge(*at(l, "act_lo", f * 22 + k + 1))) if s < 3 and reps == 1 else None)
                for s in range(12):
                    down(0, s, 1)
                for s in range(12):
                    down(1, s, 1)
                output_norm(l, q)

            def output_norm(l, q):
                pe.wait_ge(*at(l, "y_acc", 8 * q + 8))
                pe.matmul(NORM, ones, y_acc[:, :], start=True, stop=False)
                pe.wait_ge(*at(l, "y_sq", 8 * q + 8))
                pe.matmul(NORM, ones, y_sq[:, 1, :], start=False, stop=True).then_inc(*sig("y_sum"))
                keep_warm(WARM)

            def keep_warm(times):
                for _ in range(times):
                    pe.matmul(mb[0][:, 0:TP], ones, const("ones", TP), start=True, stop=True)

            def after(l, **counts):
                pe.wait_ge(setup, 16 * 3)
                for name, k in counts.items():
                    pe.wait_ge(*at(l, name, k))

            def rows(i):
                return slice(CH * i, CH * (i + 1))

            def gla_level(l, i):
                if i == 0:
                    after(l, b_qb0=1)
                    k_in, q_in = proj[:, BK, :], q_heads
                else:
                    after(l, b_kt=i, b_qbl=i)
                    k_in, q_in = lv[:, 4 + i % 2, :], q_lv
                if i >= 2:
                    after(l, b_msk=i - 1)
                for c in range(4):
                    mm = pe.matmul(ub[2 + i % 2][rows(c % 2), (c // 2) * TP:(c // 2 + 1) * TP], k_in[:, c * CH:(c + 1) * CH],
                                   q_in[:, :, c * CH:(c + 1) * CH], start=True, stop=True)
                mm.then_inc(*sig("b_sc"))

            def transposes(bank, src, name):
                for g in range(2):
                    for j in range(2):
                        mm = pe.transpose(bank[:, (2 * g + j) * P:(2 * g + j + 1) * P], src[:, j, g * P:(g + 1) * P], ident)
                mm.then_inc(*sig(name))

            def gla_tokens(l):
                after(l, proj=12)
                transposes(mb[0], proj[:, BV:BV + 2, :], "b_vT")
                after(l, b_kt=7)
                for g in range(2):
                    mm = pe.transpose(mb[1][:, g * P:(g + 1) * P], lv[:, 5, g * P:(g + 1) * P], ident)
                mm.then_inc(*sig("b_kdT"))

            def gla_updates(l):
                after(l, b_vx=2)
                for j in range(2):
                    mm = pe.matmul(mb[2][:, :], const("hvt", P * 2)[:, j * P:(j + 1) * P], v_diag[:, j * TD:(j + 1) * TD, :], start=j == 0, stop=j == 1)
                mm.then_inc(*sig("b_vb"))
                after(l, b_vt=1, b_kdt=1, b_msk=7)
                for c in range(4):
                    mm = pe.matmul(ub[2 + c % 2][:, (c // 2) * TP:(c // 2 + 1) * TP], kdt[rows(c % 2), c // 2, :], vtok[rows(c % 2), c // 2, :],
                                   start=True, stop=True)
                mm.then_inc(*sig("b_kv"))

            def gla_outputs(l):
                after(l, b_S=3, b_asc=6, b_qe=1)
                qe = proj[:, BQ, :]
                for c in (1, 0, 3, 2):
                    for j in range(2):
                        out = mb[c % 2][:, (c // 2 * 2 + j) * CH:(c // 2 * 2 + j + 1) * CH]
                        if c:
                            pe.matmul(out, state[:, c - 1, j * P:(j + 1) * P], qe[:, c * CH:(c + 1) * CH], start=True, stop=False)
                        for i in range(2):
                            h = 2 * j + i
                            mm = pe.matmul(out[rows(i), :], vtok[rows(c % 2), c // 2, h * DV:(h + 1) * DV],
                                           scores[rows(c % 2), (c // 2 * H + h) * CH:(c // 2 * H + h + 1) * CH], start=c == 0, stop=True)
                mm.then_inc(*sig("b_o"))
                after(l, b_prod=1)
                for b in range(TD):
                    for i in range(2):
                        mm = pe.matmul(mb[2][rows(i), 2 * b:2 * b + 2], st_tmp[:, b, :], const("hv", H * DV)[:, i * DV::2 * DV], start=True, stop=True)
                mm.then_inc(*sig("b_od"))

            def gla_norm(l):
                after(l, b_osq=1, d_sm=2)
                for j in range(2):
                    mm = pe.matmul(mb[j][:, 0:NT], blk, o_sq[:, j, :], start=True, stop=True)
                mm.then_inc(*sig("b_gn"))

            def conv_sum(l):
                after(l, a_all=2, a_db=1, d_sm=4)
                for c in range(2):
                    mm = pe.matmul(ub[2][:, 0:NT], ones, ymix[:, YA + c, :], start=c == 0, stop=c == 1)
                mm.then_inc(*sig("a_sum"))

            def conv_var(l):
                after(l, a_sq=1)
                for c in range(2):
                    mm = pe.matmul(ub[3][:, 0:NT], ones, a_sqr[:, c, :], start=c == 0, stop=c == 1)
                mm.then_inc(*sig("a_var"))

            def fox_scores(l, h):
                after(l, d_qm=2, d_cf=2, proj=16, b_og=3)
                for out, q0, n in ((fox_bank[h][:, 0:P], 0, P), (fox_bank[h][:, P:3 * P], P, TP)):
                    pe.matmul(out, qm[:, h, q0:q0 + P], proj[:, DKK + h // 2, 0:n], start=True, stop=False)
                    mm = pe.matmul(out, const("sel", H * P, H)[:, h * P:(h + 1) * P], cf[:, 0:n], start=False, stop=True)
                mm.then_inc(*sig("d_sc"))

            def fox_transposes(l, h):
                after(l, d_pn=2, b_rs=2)
                if h >= 2:
                    after(l, d_pt=h - 1)
                for i in range(3):
                    mm = pe.transpose(mb[h % 2][:, i * P:(i + 1) * P], sm[:, h, i * P:(i + 1) * P], ident)
                mm.then_inc(*sig("d_pT"))

            def fox_outputs(l):
                after(l, d_pt=4, d_vt=1)
                for h in range(H):
                    out = mb[2][rows(h % 2), h // 2 * TP:(h // 2 + 1) * TP]
                    pe.matmul(out, vtok[:, 0, h * DV:(h + 1) * DV], smT[:, h, 0:TP], start=True, stop=False)
                    mm = pe.matmul(out[:, P:TP], vtok[:, 1, h * DV:(h + 1) * DV], smT[:, h, TP:3 * P], start=False, stop=True)
                mm.then_inc(*sig("d_o"))

            def decode_scores(l, group):
                after(l, d_qm=2, keys_in=256)
                out = mb[3][:, 0:64].rearrange("p (g h b) -> p g h b", g=NPAGES, h=H)
                for b in range(4):
                    for j in range(2):
                        for g in range(NPAGES):
                            mm = pe.matmul(out[:, g, 2 * j:2 * j + 2, 4 * group + b], pages[:, (4 * group + b) * NPAGES + g, j * P:(j + 1) * P],
                                           qm[:, 2 * j:2 * j + 2, TP + 4 * group + b], start=True, stop=True)
                mm.then_inc(*sig("d_dsc"))

            def decode_new(l):
                after(l, d_pm=2, d_scs=1)
                pe.matmul(mb[3][0:32, 320:321], pm[:, :, :].rearrange("p h b -> p (h b)"), ones[:, 0:1], start=True, stop=True)\
                  .then_inc(*sig("d_new"))

            def decode_transposes(l):
                after(l, d_scs=1)
                for g in range(NPAGES):
                    mm = pe.transpose(mb[3][0:32, 64 + g * P:64 + (g + 1) * P], sct[:, 32 * g:32 * (g + 1)], ident)
                mm.then_inc(*sig("d_dT"))

            def decode_back(l):
                after(l, d_dp=2)
                for g in range(NPAGES):
                    pe.transpose(mb[3][:, 384 + 32 * g:384 + 32 * (g + 1)], sd[:, g * PAGE:(g + 1) * PAGE], ident[0:32, 0:32])
                for j in range(2):
                    mm = pe.matmul(mb[3][:, 480 + TD * j:480 + TD * (j + 1)], const("heads", 2 * P, 32)[:, j * P:(j + 1) * P], p_new[:, :],
                                   start=True, stop=True)
                mm.then_inc(*sig("d_dpT"))

            def decode_outputs(l, sequences):
                after(l, d_ptd=1, **{"values_in0" if sequences[-1] < 4 else "values_in1": 128})
                for b in sequences:
                    for j in range(2):
                        col = 448 + (j * TD + b) * 2
                        for g in range(NPAGES):
                            mm = pe.matmul(mb[3][:, col:col + 2], pages[:, b * NPAGES + g, j * P:(j + 1) * P],
                                           ptd[:, g, 2 * j:2 * j + 2, b], start=g == 0, stop=g == 1)
                mm.then_inc(*sig("d_dpv"))

            def mix(l, n):
                if n == 4:
                    after(l, proj=1)
                    pe.matmul(mb[2][:, 0:NT], par[0:16, PAR["wa2"]:PAR["wa2"] + P], proj[0:16, ALR, :], start=True, stop=True).then_inc(*sig("b_z"))
                if 6 <= n <= 12:
                    gla_level(l, n - 6)
                if n == 13:
                    gla_tokens(l)
                if n == 14:
                    gla_updates(l)
                    decode_scores(l, 0)
                if n == 15:
                    decode_scores(l, 1)
                if n == 16:
                    gla_outputs(l)
                if n == 17:
                    decode_new(l)
                    decode_transposes(l)
                if n == 18:
                    fox_scores(l, 0)
                    fox_scores(l, 1)
                if n == 19:
                    fox_scores(l, 2)
                    fox_scores(l, 3)
                    after(l, proj=18, b_og=3)
                    transposes(mb[2], proj[:, DVV:DVV + 2, :], "d_vT")
                if n == 20:
                    gla_norm(l)
                    decode_back(l)
                if n == 21:
                    decode_outputs(l, (0, 1, 2, 3))
                    conv_sum(l)
                if n == 22:
                    for h in range(H):
                        fox_transposes(l, h)
                if n == 23:
                    conv_var(l)
                    fox_outputs(l)
                    decode_outputs(l, (4, 5, 6, 7))

            def mixer(l):
                multiply_first(pe, l, "in", hg_hi, hg_lo, ub, IN_WIDTH, "hg_ready", 0)
                pe.wait_ge(*at(l, "h_acc", 9))
                pe.matmul(NORM, ones, h_acc[:, :], start=True, stop=True).then_inc(*sig("h_sum"))
                for n in range(GROUP, 24):
                    pe.wait_ge(S["split_done"], l * UNITS + PHASES["in"][0] + n + 1 + RING)
                    if n >= 4:
                        pe.wait_ge(*at(l, "proj", {4: 1, 5: 2}.get(n, n - 1)))
                    multiply_unit(pe, unit_bank(n)[:, 0:NT], n % RING, hg_hi, hg_lo, KD, 0, True, True, 1)
                    mix(l, n)
                pe.wait_ge(*at(l, "proj", 24))
                pe.wait_ge(*at(l, "a_cen", 2))
                multiply_first(pe, l, "out", ym_hi, ym_lo, ub, [P] * GROUP, "ym_ready", 0)
                for n in range(GROUP, KD):
                    pe.wait_ge(S["split_done"], l * UNITS + PHASES["out"][0] + n + 1 + RING)
                    if n >= 4:
                        pe.wait_ge(*at(l, "y_scaled", 8 + n - 3))
                    multiply_unit(pe, ub[n % 4][:, 0:NT], n % RING, ym_hi, ym_lo, KD, 0, True, True, 1)
                output_norm(l, 1)

            with pe.Fori(0, L) as l:
                feed_forward(l, 0)
                mixer(l)
                feed_forward(l, 2)

        @block.scalar
        def _(act):
            def input_tile(l, q, k, gain):
                act.activation(hg_hi[:, k, :], resid[:, k, :], ACT.Copy, scale=gain[:, k:k + 1]).then_inc(*sig("hg_hi"))
                if k >= 2:
                    act.wait_ge(*at(l, "h_acc", 9 * q + k))
                act.activation(h_sq[:, k % 2, :], resid[:, k, :], ACT.Square).then_inc(*sig("h_sq"))

            def output_tile(l, q, n, bank, b, reps):
                act.wait_ge(*at(l, "y_acc", 8 * q + n))
                act.activation(y_sq[:, b, :], bank[:, 0:NT], ACT.Square).then_inc(*sig("y_sq", reps))
                act.activation(yg[:, n, :] if isinstance(n, int) else yg[:, bass.ds(n, 1), :].rearrange("p a c -> p (a c)"),
                               bank[:, 0:NT], ACT.Copy,
                               scale=par[:, PAR["post"] + q * 8 + n:PAR["post"] + q * 8 + n + 1] if isinstance(n, int)
                               else par[:, bass.ds(PAR["post"] + q * 8 + n, 1)]).then_inc(*sig("y_scaled", reps))

            def rsqrt(l, name, k, out, total, scale, **bias):
                act.activation(ln_t[:, :], total, ACT.Ln, bias=biases[:, 0:1], scale=scale).then_inc(*sig(name))
                act.wait_ge(*at(l, name, k + 1))
                act.activation(out, ln_t[:, :], ACT.Exp, scale=-0.5, **bias).then_inc(*sig(name))

            def input_norm(l, q):
                act.wait_ge(*at(l, "h_sum", q + 1))
                rsqrt(l, "rh_ready", 2 * q, rs_h[:, :], NORM, 1.0 / D)

            def boundary(l, q):
                act.wait_ge(*at(l, "y_sum", q + 1))
                half = {} if q == 1 else {"bias": biases[:, 1:2]}
                rsqrt(l, "ry_ready", 2 * q, rs_y[:, :], NORM, 1.0 / D, **half)
                for k in range(KD):
                    act.wait_ge(*at(l, "h_ready", 8 * q + k + 1))
                    input_tile(l, q, k, par[:, PAR["pre"] + 8 * q:PAR["pre"] + 8 * q + 8])

            def feed_forward(l, q):
                f = q // 2
                gu, dn = f"gu{f}", f"dn{f}"

                def gate_up(i, s, reps, lead):
                    round_unit(act, lead, reps)
                    if isinstance(i, int) and i == 0 and s == 1:
                        input_norm(l, q)
                        act.preload_act_table(ACT.Silu)
                    if s % 2:
                        j, b = i * 2 + s // 2, s // 2
                        act.wait_ge(*at(l, "gu_read", f * 44 + 2 * j + 1))
                        act.activation(silu_s[:, b, :], gate_s[:, b, :], ACT.Silu).then_inc(*sig("silu_ready", reps))
                        if not (isinstance(i, int) and j == 0):
                            round_act(j - 1, 1 - b, reps)

                def round_act(j, b, reps):
                    act.wait_ge(*at(l, "act_ready", f * 22 + j + 1))
                    act.activation(tile_of(act_hi, j), act_s[:, b, :], ACT.Copy).then_inc(*sig("act_hi", reps))
                steps(act, gu, l, gate_up, peel_first=True)
                round_act(21, 1, 1)
                act.preload_act_table_set("natural_log_exp_and_others")

                def down(i, s, reps, lead):
                    round_unit(act, lead, reps)
                    if s % 3 == 2:
                        n, b = i * 4 + s // 3, s // 3 % 2
                        act.wait_ge(S["unit_done"], l * UNITS + PHASES[dn][0] + i * 12 + s + 1 + RING)
                        output_tile(l, q, n, ub[b], b, reps)
                steps(act, dn, l, down, 12)
                boundary(l, q)

            def after(l, **counts):
                for name, k in counts.items():
                    act.wait_ge(*at(l, name, k))

            def rows(i):
                return slice(CH * i, CH * (i + 1))

            def softplus(l, out, x, bias, name):
                act.activation(out, x, ACT.Abs, bias=bias).then_inc(*sig(name))
                after(l, **{name: 1})
                act.activation(out, out, ACT.Exp, scale=-1.0).then_inc(*sig(name))
                after(l, **{name: 2})
                act.activation(out, out, ACT.Ln, bias=biases[0:out.shape[0], 2:3]).then_inc(*sig(name))

            def level_decays(l, i):
                after(l, b_D=2 * i if i < 7 else 13)
                if i >= 3:
                    after(l, b_kt=i - 2, b_qbl=i - 2)
                act.activation(lv[:, 2 + i % 2, :], lv[:, i % 2, :], ACT.Exp, scale=1 / GLA_TAU).then_inc(*sig("b_E"))

            def mix(l, n):
                if n == 5:
                    after(l, b_z=1)
                    softplus(l, soft[:, :], mb[2][:, 0:NT], par[:, PAR["ba"]:PAR["ba"] + 1], "b_sp")
                if n == 8:
                    after(l, proj=2)
                    softplus(l, lft[:, :], proj[0:H, FG, :], par[0:H, PAR["bf"]:PAR["bf"] + 1], "d_sp")
                if n == 4:
                    after(l, proj=3)
                    act.activation(proj[:, BQ, :], proj[:, BQ, :], ACT.Copy, scale=DK ** -0.5).then_inc(*sig("b_qs"))
                if n == 6:
                    after(l, b_bc=2)
                    act.activation(eb[:, :], bc[:, :], ACT.Exp, scale=1 / GLA_TAU).then_inc(*sig("b_eb"))
                    level_decays(l, 1)
                if 7 <= n <= 12:
                    level_decays(l, n - 5)
                if n == 10:
                    act.preload_act_table(ACT.Sigmoid)
                    after(l, proj=10)
                    act.activation(proj[:, AG:AG + 2, :], proj[:, AG:AG + 2, :], ACT.Sigmoid).then_inc(*sig("a_sg"))
                    act.activation(sg[:, :, :], proj[:, BG:BG + 2, :], ACT.Sigmoid).then_inc(*sig("b_sg"))
                    act.preload_act_table_set("natural_log_exp_and_others")
                if n == 14:
                    after(l, b_vT=1)
                    act.activation(vtok[:, :, :].rearrange("p a b -> p (a b)"), mb[0][:, :], ACT.Copy).then_inc(*sig("b_vt"))
                    after(l, b_kdT=1)
                    act.activation(kdt[:, :, :].rearrange("p a b -> p (a b)"), mb[1][:, 0:TP], ACT.Copy).then_inc(*sig("b_kdt"))
                if n == 14:
                    after(l, proj=14, d_qz=1)
                    for i in range(2):
                        act.activation(qm[rows(i), i::2, :], proj[rows(i), DQ:DQ + 2, :], ACT.Copy).then_inc(*sig("d_qm"))
                if n == 16:
                    after(l, d_dsc=2)
                    act.activation(sct[:, :], mb[3][:, 0:64], ACT.Copy).then_inc(*sig("d_scs"))
                if n == 17:
                    after(l, b_o=1)
                    o = ymix[:, YB:YB + 2, 0:TP].rearrange("p j (g c t) -> p j g c t", g=2, c=2)
                    for c in range(2):
                        act.activation(o[:, :, :, c, :].rearrange("p j g t -> p g j t"), mb[c][:, 0:TP].rearrange("p (g j t) -> p g j t", g=2, j=2),
                                       ACT.Copy).then_inc(*sig("b_og"))
                    after(l, b_od=1)
                    act.activation(ymix[:, YB:YB + 2, TP:NT], mb[2][:, 0:16].rearrange("p (b j) -> p j b", j=2), ACT.Copy).then_inc(*sig("b_og"))
                if n == 18:
                    after(l, b_og=3)
                    act.activation(o_sq[:, :, :], ymix[:, YB:YB + 2, :], ACT.Square).then_inc(*sig("b_osq"))
                if n == 20:
                    after(l, d_vT=1)
                    act.activation(vtok[:, :, :].rearrange("p a b -> p (a b)"), mb[2][:, :], ACT.Copy).then_inc(*sig("d_vt"))
                if n == 19:
                    after(l, d_dmx=1)
                    act.activation(sd[:, :], sd[:, :], ACT.Exp, bias=dstat[:, 1:2], accum_out=dstat[:, 2:3]).then_inc(*sig("d_dex"))
                if n == 21:
                    after(l, d_dpT=1)
                    act.activation(ptd[:, :, :, :].rearrange("p g h b -> p (g h b)"), mb[3][:, 384:448], ACT.Copy).then_inc(*sig("d_ptd"))
                    after(l, b_gn=1)
                    for j in range(2):
                        act.activation(o_rs[:, j, :], mb[j][:, 0:NT], ACT.Ln, bias=biases[:, 0:1], scale=1.0 / DV).then_inc(*sig("b_rs"))
                    for j in range(2):
                        after(l, b_rs=j + 1)
                        act.activation(o_rs[:, j, :], o_rs[:, j, :], ACT.Exp, scale=-0.5).then_inc(*sig("b_rs"))
                    after(l, d_mx=2)
                    for h in range(H):
                        for b, part in ((0, slice(0, P)), (1, slice(P, 3 * P))):
                            act.activation(sm[:, h, part], sm[:, h, part], ACT.Exp, bias=stats[:, 0, b * H + h:b * H + h + 1],
                                           accum_out=stats[:, 1, b * H + h:b * H + h + 1]).then_inc(*sig("d_ex"))
                if n == 22:
                    round_mixed(l, YB)
                    after(l, a_cen=2, b_t=2)
                    act.activation(a_sqr[:, :, :], ymix[:, YA:YA + 2, :], ACT.Square).then_inc(*sig("a_sq"))
                    for h in range(H):
                        probabilities(l, h)
                if n == 23:
                    after(l, a_var=1)
                    act.activation(a_rs[:, :], ub[3][:, 0:NT], ACT.Ln, bias=biases[:, 0:1], scale=1.0 / 256).then_inc(*sig("a_rsd"))
                    after(l, a_rsd=1)
                    act.activation(a_rs[:, :], a_rs[:, :], ACT.Exp, scale=-0.5).then_inc(*sig("a_rsd"))
                    act.preload_act_table(ACT.Silu)
                    after(l, d_o=1)
                    act.activation(ymix[:, YD:YD + 2, 0:TP], mb[2][:, :].rearrange("p (a b) -> p a b", a=2), ACT.Copy).then_inc(*sig("d_y"))
                    after(l, a_nrm=1)
                    for c in range(2):
                        act.activation(ymix[:, YA + c, :], ymix[:, YA + c, :], ACT.Silu, scale=par[:, PAR["alg"] + c:PAR["alg"] + c + 1],
                                       bias=par[:, PAR["alb"] + c:PAR["alb"] + c + 1]).then_inc(*sig("a_y"))

            def round_mixed(l, first):
                after(l, **{YB: dict(b_y=1), YA: dict(a_y=2), YD: dict(d_y=1, d_dy=2), YC: dict(c_y=1, c_y1=1)}[first])
                for k in (first, first + 1):
                    act.activation(ym_hi[:, k, :], ymix[:, k, :], ACT.Copy).then_inc(*sig("ym_hi"))

            def probabilities(l, h):
                after(l, d_pT=h + 1)
                act.activation(smT[:, h, :], mb[h % 2][:, 0:3 * P], ACT.Copy).then_inc(*sig("d_pt"))

            def mixer(l):
                def inp(i, s, reps, lead):
                    round_unit(act, lead, reps)
                    if s == 1:
                        input_norm(l, 1)
                    mix(l, s)
                steps(act, "in", l, inp, 24)
                def outp(i, n, reps, lead):
                    round_unit(act, lead, reps)
                    if n == 0:
                        act.preload_act_table_set("natural_log_exp_and_others")
                    act.wait_ge(S["unit_done"], l * UNITS + PHASES["out"][0] + n + 1 + RING)
                    output_tile(l, 1, n, ub[n % 4], n % 2, reps)
                for first in range(2, KD, 2):
                    round_mixed(l, first)
                steps(act, "out", l, outp, 8)
                boundary(l, 1)

            act.preload_act_table_set("natural_log_exp_and_others")
            act.wait_ge(started, 3)
            for k in range(KD):
                act.wait_ge(x_in[k], 16 * (1 + (k == 0)))
                if k < LEAD:
                    round_unit(act, first_unit(k), 0)
                act.activation(hg_hi[:, k, :], resid[:, k, :], ACT.Copy, scale=gain0[:, k:k + 1]).then_inc(S["hg_hi"], 1)
                if k >= 2:
                    act.wait_ge(S["h_acc"], k)
                act.activation(h_sq[:, k % 2, :], resid[:, k, :], ACT.Square).then_inc(S["h_sq"], 1)
            with act.Fori(0, L) as l:
                act.wait_ge(*at(l, "par_ready", 1))
                feed_forward(l, 0)
                mixer(l)
                feed_forward(l, 2)

        @block.vector
        def _(dve):
            def input_rest(l, q, k, gain):
                dve.wait_ge(*at(l, "hg_hi", 8 * q + k + 1))
                dve.scalar_tensor_tensor(hg_lo[:, k, :], resid[:, k, :], gain[:, k:k + 1], hg_hi[:, k, :].bitcast(F32),
                                         ALU.mult, ALU.subtract).then_inc(*sig("hg_ready"))

            def boundary(l, q):
                dve.wait_ge(*at(l, "ry_ready", 2 * q + 2))
                for k in range(KD + 2):
                    if k < KD:
                        dve.wait_ge(*at(l, "y_scaled", 8 * q + k + 1))
                        if k >= 2:
                            dve.wait_ge(*at(l, "h_ready", 8 * q + k - 1))
                        dve.tensor_tensor(z_t[:, k % 2, :], yg[:, k, :], rs_y[:, :], ALU.mult).then_inc(*sig("z_ready"))
                    if 1 <= k <= KD:
                        dve.wait_ge(*at(l, "z_ready", 8 * q + k))
                        dve.tensor_tensor(resid[:, k - 1, :], resid[:, k - 1, :], z_t[:, (k - 1) % 2, :], ALU.add)\
                           .then_inc(*sig("h_ready"))
                    if k >= 2:
                        input_rest(l, q, k - 2, par[:, PAR["pre"] + 8 * q:PAR["pre"] + 8 * q + 8])

            def feed_forward(l, q):
                f = q // 2
                gu, dn = f"gu{f}", f"dn{f}"

                def gate_up(i, s, reps, lead):
                    j, b = i * 2 + s // 2, s // 2
                    rest_unit(dve, lead, reps)
                    if s == 1:
                        dve.wait_ge(*at(l, "rh_ready", 2 * q + 2))
                    if s % 2:
                        dve.wait_ge(S["unit_done"], l * UNITS + PHASES[gu][0] + i * 4 + s + RING)
                        dve.wait_ge(*at(l, "silu_ready", f * 22 + j - 1))
                        dve.tensor_tensor(gate_s[:, b, :], ub[s - 1][:, 0:NT], rs_h[:, :], ALU.mult)\
                           .then_inc(*sig("gu_read", reps))
                        dve.wait_ge(S["unit_done"], l * UNITS + PHASES[gu][0] + i * 4 + s + 1 + RING)
                        dve.wait_ge(*at(l, "act_ready", f * 22 + j - 1))
                        dve.tensor_tensor(up_s[:, b, :], ub[s][:, 0:NT], rs_h[:, :], ALU.mult)\
                           .then_inc(*sig("gu_read", reps))
                steps(dve, gu, l, gate_up)
                steps(dve, dn, l, lambda i, s, reps, lead: rest_unit(dve, lead, reps), 12)
                boundary(l, q)

            def after(l, **counts):
                for name, k in counts.items():
                    dve.wait_ge(*at(l, name, k))

            def log_sigmoid(l, out, x, bias, minus, name):
                dve.tensor_scalar(out, x, bias, 0.0, ALU.add, ALU.min).then_inc(*sig(name))
                after(l, **{name: 1})
                dve.tensor_tensor(out, out, minus, ALU.subtract).then_inc(*sig(name))

            def level_exponents(l, i):
                if i >= 3:
                    after(l, b_E=i - 2)
                out = lv[:, i % 2, :]
                if i == 7:
                    b, out = (t.rearrange("p (n m) -> p n m", m=CH) for t in (bc[:, 0:TP], out))
                    dve.tensor_tensor(out, b[:, :, CH - 1:CH].to_broadcast([P, TP // CH, CH]), b, ALU.subtract).then_inc(*sig("b_D"))
                    return
                m = LEVELS[i]
                b, out = (t.rearrange("p (n two m) -> p n two m", two=2, m=m) for t in (bc[:, 0:TP], out))
                mid = b[:, :, 0, m - 1:m].to_broadcast([P, TP // (2 * m), m])
                dve.tensor_tensor(out[:, :, 0, :], mid, b[:, :, 0, :], ALU.subtract).then_inc(*sig("b_D"))
                dve.tensor_tensor(out[:, :, 1, :], b[:, :, 1, :], mid, ALU.subtract).then_inc(*sig("b_D"))

            def level_keys(l, i):
                after(l, b_E=i, proj=4)
                if i >= 3:
                    after(l, b_sc=i - 1)
                dve.tensor_tensor(lv[:, 4 + i % 2, :], proj[:, BK, 0:TP], lv[:, 2 + i % 2, :], ALU.mult).then_inc(*sig("b_kt"))

            def level_mask(l, i):
                after(l, b_sc=i + 1)
                if i >= 2:
                    after(l, b_asc=i - 1)
                out = (level if i else scores)[:, :].rearrange("p (a t) -> p a t", t=CH)
                mask = const("lvm", 7 * CH)[:, i * CH:(i + 1) * CH].unsqueeze(1).to_broadcast([P, 8, CH])
                dve.tensor_tensor(out, ub[2 + i % 2][:, :].rearrange("p (a t) -> p a t", t=CH), mask, ALU.mult).then_inc(*sig("b_msk"))
                if i:
                    after(l, b_msk=i + 1)
                    dve.tensor_tensor(scores[:, :], scores[:, :], level[:, :], ALU.add).then_inc(*sig("b_asc"))

            def conv_taps(l, first, last):
                for t in range(first, last):
                    for c in range(2):
                        k = 2 * t + c
                        y, x, w = ymix[:, YA + c, 0:TP], a_pad[:, c, t:t + TP], par[:, PAR["acw"] + c * TAPS_A + t:PAR["acw"] + c * TAPS_A + t + 1]
                        if t == 0:
                            dve.tensor_scalar(y, x, w, par[:, PAR["acb"] + c:PAR["acb"] + c + 1], ALU.mult, ALU.add).then_inc(*sig("a_tap"))
                        else:
                            after(l, a_tap=k - 1)
                            dve.scalar_tensor_tensor(y, x, w, y, ALU.mult, ALU.add).then_inc(*sig("a_tap"))

            def mix(l, n):
                if n == 5:
                    after(l, b_z=1, b_sp=3)
                    log_sigmoid(l, la[:, :], mb[2][:, 0:NT], par[:, PAR["ba"]:PAR["ba"] + 1], soft[:, :], "b_la")
                    after(l, b_la=2)
                    dve.tensor_tensor_scan(bc[:, 0:TP], const("rst", TP), la[:, 0:TP], 0.0, ALU.mult, ALU.add).then_inc(*sig("b_bc"))
                    dve.tensor_copy(bc[:, TP:NT], la[:, TP:NT]).then_inc(*sig("b_bc"))
                    after(l, b_bc=2)
                    level_exponents(l, 1)
                    level_exponents(l, 2)
                if n == 8:
                    after(l, d_sp=3, proj=2)
                    log_sigmoid(l, lf[:, :], proj[0:H, FG, :], par[0:H, PAR["bf"]:PAR["bf"] + 1], lft[:, :], "d_lf")
                    after(l, d_lf=2)
                    dve.tensor_tensor_scan(cf[:, 0:TP], const("ones", TP, H), lf[:, 0:TP], 0.0, ALU.mult, ALU.add).then_inc(*sig("d_cf"))
                    after(l, d_cf=1)
                    dve.tensor_scalar(cf[:, 0:TP], cf[:, 0:TP], -8.0, None, ALU.mult).then_inc(*sig("d_cf"))
                if 6 <= n <= 12:
                    if n <= 10:
                        level_exponents(l, n - 3)
                    level_keys(l, n - 5)
                if 7 <= n <= 13:
                    level_mask(l, n - 7)
                if n == 12:
                    after(l, a_in=2)
                if n == 15:
                    after(l, b_kv=1, b_vb=1)
                    for c in range(2):
                        dve.tensor_tensor(state[:, c::2, :], ub[2 + c][:, :].rearrange("p (g v) -> p g v", g=2),
                                          const("hv", H * DV).unsqueeze(1).to_broadcast([P, 2, H * DV]), ALU.mult).then_inc(*sig("b_kvm"))
                    after(l, b_kvm=2)
                    for c in range(1, 4):
                        if c > 1:
                            after(l, b_S=c - 1)
                        dve.scalar_tensor_tensor(state[:, c, :], state[:, c - 1, :], eb[:, (c + 1) * CH - 1:(c + 1) * CH], state[:, c, :],
                                                 ALU.mult, ALU.add).then_inc(*sig("b_S"))
                    dve.tensor_tensor(st_tmp[:, :, :], mb[2][:, :].rearrange("p (b v) -> p b v", v=DV),
                                      proj[:, BK, TP:NT].unsqueeze(2).to_broadcast([P, TD, DV]), ALU.mult).then_inc(*sig("b_kvd"))
                if n == 16:
                    after(l, b_sd=1)
                    dve.tensor_tensor(st_tmp[:, :, :], st[:, :, :], proj[:, BQ, TP:NT].unsqueeze(2).to_broadcast([P, TD, DV]), ALU.mult)\
                       .then_inc(*sig("b_prod"))
                if n == 16:
                    after(l, past=PAST, lfn_in=16)
                    dve.tensor_tensor_scan(tail[:, :], const("ones", TP, H * TD), lfp[:, :], 0.0, ALU.mult, ALU.add).then_inc(*sig("d_ct"))
                    after(l, d_ct=1)
                    dve.tensor_tensor(dstat[:, 0:1], tail[:, TP - 1:TP], lfn[:, :], ALU.add).then_inc(*sig("d_ct"))
                    after(l, d_ct=2)
                    dve.tensor_scalar(tail[:, :], tail[:, :], -1.0, dstat[:, 0:1], ALU.mult, ALU.add).then_inc(*sig("d_ct"))
                if n == 18:
                    after(l, a_dp=2)
                    dve.tensor_reduce(ymix[:, YA:YA + 2, TP:NT], a_prod[:, :, :, :], AX.X, ALU.add).then_inc(*sig("a_dr"))
                    after(l, a_dr=1)
                    dve.tensor_tensor(ymix[:, YA:YA + 2, TP:NT], ymix[:, YA:YA + 2, TP:NT],
                                      par[:, PAR["acb"]:PAR["acb"] + 2].unsqueeze(2).to_broadcast([P, 2, TD]), ALU.add).then_inc(*sig("a_db"))
                if n in (19, 20):
                    for h in (2 * (n - 19), 2 * (n - 19) + 1):
                        biased(l, h)
                if n == 20:
                    after(l, d_sm=4)
                    dve.tensor_reduce(stats[:, 0, 0:H], sm[:, :, 0:P], AX.X, ALU.max, negate=True).then_inc(*sig("d_mx"))
                    dve.tensor_reduce(stats[:, 0, H:2 * H], sm[:, :, P:3 * P], AX.X, ALU.max, negate=True).then_inc(*sig("d_mx"))
                if n == 18:
                    after(l, d_dT=1, d_new=1, d_ct=3)
                    dve.scalar_tensor_tensor(sd[:, 0:TP], mb[3][0:H * TD, 64:64 + TP], DV ** -0.5, tail[:, :], ALU.mult, ALU.add).then_inc(*sig("d_ds"))
                    dve.tensor_scalar(sd[:, TP:TP + 1], mb[3][0:H * TD, 320:321], DV ** -0.5, None, ALU.mult).then_inc(*sig("d_ds"))
                    after(l, d_ds=2)
                    dve.tensor_reduce(dstat[:, 1:2], sd[:, :], AX.X, ALU.max, negate=True).then_inc(*sig("d_dmx"))
                if n == 19:
                    after(l, d_dex=1)
                    dve.reciprocal(dstat[:, 3:4], dstat[:, 2:3]).then_inc(*sig("d_dri"))
                    after(l, d_dri=1)
                    dve.tensor_scalar(sd[:, :], sd[:, :], dstat[:, 3:4], None, ALU.mult).then_inc(*sig("d_dp"))
                    after(l, d_dp=1)
                    dve.tensor_scalar(p_new[:, :], const("dec", TD, H * TD), sd[:, TP:TP + 1], None, ALU.mult).then_inc(*sig("d_dp"))
                if n in TAPS:
                    conv_taps(l, *TAPS[n])
                if n == 20:
                    after(l, a_tap=2 * A_DVE, a_ptap=2 * (TAPS_A - A_DVE))
                    for c in range(2):
                        dve.tensor_tensor(ymix[:, YA + c, 0:TP], ymix[:, YA + c, 0:TP], a_part[c][:, 0:TP], ALU.add).then_inc(*sig("a_all"))
                if n == 21:
                    after(l, b_rs=4, b_gs=1)
                    for j in range(2):
                        dve.scalar_tensor_tensor(o_rs[:, j, :], sg[:, j, :], par[:, PAR["bng"] + j:PAR["bng"] + j + 1], o_rs[:, j, :],
                                                 ALU.mult, ALU.mult).then_inc(*sig("b_t"))
                    after(l, b_t=2)
                    dve.tensor_tensor(ymix[:, YB:YB + 2, :], ymix[:, YB:YB + 2, :], o_rs[:, :, :], ALU.mult).then_inc(*sig("b_y"))
                    after(l, d_ex=8)
                    dve.reciprocal(stats[:, 2, :], stats[:, 1, :]).then_inc(*sig("d_ri"))
                    after(l, d_ri=1)
                    for b, part in ((0, slice(0, P)), (1, slice(P, 3 * P))):
                        dve.tensor_tensor(sm[:, :, part], sm[:, :, part],
                                          stats[:, 2, b * H:(b + 1) * H].unsqueeze(2).to_broadcast([P, H, P * (b + 1)]), ALU.mult).then_inc(*sig("d_pn"))
                if n == 22:
                    rest_mixed(l, YB)
                    after(l, a_sum=1)
                    for c in range(2):
                        dve.scalar_tensor_tensor(ymix[:, YA + c, :], ub[2][:, 0:NT], -1.0 / 256, ymix[:, YA + c, :], ALU.mult, ALU.add)\
                           .then_inc(*sig("a_cen"))
                if n == 24:
                    after(l, a_rsd=2)
                    dve.tensor_tensor(ymix[:, YA:YA + 2, :], ymix[:, YA:YA + 2, :], a_rs[:, :].unsqueeze(1).to_broadcast([P, 2, NT]), ALU.mult)\
                       .then_inc(*sig("a_nrm"))
                    z, y = z_pad[:, 1, :], ymix[:, YC + 1, :]
                    w = [par[:, PAR["ccw"] + TAPS_C + t:PAR["ccw"] + TAPS_C + t + 1] for t in range(TAPS_C)]
                    after(l, proj=24, b_y=1)
                    dve.memset(z[:, 0:2], 0.0).then_inc(*sig("c_z1"))
                    dve.tensor_tensor(z[:, 2:], proj[:, CC + 3, 0:TP], proj[:, CX + 3, 0:TP], ALU.mult).then_inc(*sig("c_z1"))
                    dve.tensor_tensor(z_dec[:, 1, :, 2], proj[:, CC + 3, TP:NT], proj[:, CX + 3, TP:NT], ALU.mult).then_inc(*sig("c_z1"))
                    after(l, c_z1=3)
                    for t in range(TAPS_C):
                        for y_t, z_t1 in ((y[:, 0:TP], z[:, t:t + TP]), (y[:, TP:NT], z_dec[:, 1, :, t])):
                            if t == 0:
                                dve.tensor_scalar(y_t, z_t1, w[t], None, ALU.mult).then_inc(*sig("c_t1"))
                            else:
                                dve.scalar_tensor_tensor(y_t, z_t1, w[t], y_t, ALU.mult, ALU.add).then_inc(*sig("c_t1"))
                        after(l, c_t1=2 * t + 2)
                    dve.tensor_tensor(y, y, proj[:, CB + 3, :], ALU.mult).then_inc(*sig("c_y1"))
                    after(l, d_dpv=2, proj=18)
                    dve.tensor_tensor(d_tmp[:, :].rearrange("p (j b) -> p j b", j=2), mb[3][:, 480:496].rearrange("p (j b) -> p j b", j=2),
                                      proj[:, DVV:DVV + 2, TP:NT], ALU.mult).then_inc(*sig("d_dt"))
                    after(l, d_dt=1)
                    for i in range(2):
                        r = slice(CH * i, CH * (i + 1))
                        dve.tensor_tensor(ymix[r, YD:YD + 2, TP:NT], mb[3][r, 448 + i:480:2].rearrange("p (j b) -> p j b", j=2),
                                          d_tmp[r, :].rearrange("p (j b) -> p j b", j=2), ALU.add).then_inc(*sig("d_dy"))

            def rest_mixed(l, first):
                for k in (first, first + 1):
                    dve.wait_ge(*at(l, "ym_hi", k + 1))
                    dve.tensor_tensor(ym_lo[:, k, :], ymix[:, k, :], ym_hi[:, k, :].bitcast(F32), ALU.subtract)\
                       .then_inc(*sig("ym_ready"))

            def biased(l, h):
                after(l, d_sc=h + 1)
                dve.scalar_tensor_tensor(sm[:, h, :], fox_bank[h][:, 0:3 * P], DV ** -0.5, const("tri", 3 * P), ALU.mult, ALU.add).then_inc(*sig("d_sm"))

            def mixer(l):
                def evacuate(n):
                    m = IN_WIDTH[n]
                    dve.wait_ge(S["unit_done"], l * UNITS + PHASES["in"][0] + n + 1 + RING)
                    dve.tensor_tensor(proj[0:m, n, :], unit_bank(n)[0:m, 0:NT], rs_h[0:m, :], ALU.mult).then_inc(*sig("proj"))

                def inp(i, s, reps, lead):
                    rest_unit(dve, lead, reps)
                    if s == 1:
                        dve.wait_ge(*at(l, "rh_ready", 4))
                    if s >= 1:
                        evacuate(s - 1)
                    mix(l, s)
                steps(dve, "in", l, inp, 24)
                evacuate(23)
                mix(l, 24)
                for first in range(2, KD, 2):
                    rest_mixed(l, first)
                steps(dve, "out", l, lambda i, s, reps, lead: rest_unit(dve, lead, reps), 8)
                boundary(l, 1)

            dve.memset(biases[:, 0:1], EPS).then_inc(started, 1)
            dve.memset(biases[:, 1:2], LN_HALF).then_inc(started, 1)
            dve.memset(biases[:, 2:3], 1.0).then_inc(started, 1)
            for k in range(KD):
                if k < LEAD:
                    rest_unit(dve, first_unit(k), 0)
                dve.wait_ge(S["hg_hi"], k + 1)
                dve.wait_ge(x_in[k], 16 * (1 + (k == 0)))
                dve.scalar_tensor_tensor(hg_lo[:, k, :], resid[:, k, :], gain0[:, k:k + 1], hg_hi[:, k, :].bitcast(F32),
                                         ALU.mult, ALU.subtract).then_inc(S["hg_ready"], 1)
            dve.wait_ge(setup, 16 * 3)
            with dve.Fori(0, L) as l:
                dve.wait_ge(*at(l, "hg_ready", 0))
                dve.tensor_copy(par[:, :], par_all[:, bass.ds(l, 1), :].rearrange("p a c -> p (a c)")).then_inc(*sig("par_ready"))
                feed_forward(l, 0)
                mixer(l)
                feed_forward(l, 2)

        @block.gpsimd
        def _(pool):
            def output_squares(l, q):
                pool.wait_ge(*at(l, "y_sum", q))
                pool.tensor_tensor(y_acc[:, :], con[:, 0:NT], con[:, 0:NT], ALU.subtract).then_inc(*sig("y_acc"))
                for n in range(KD - 1):
                    pool.wait_ge(*at(l, "y_sq", 8 * q + n + 1))
                    pool.wait_ge(*at(l, "y_acc", 8 * q + n + 1))
                    pool.tensor_tensor(y_acc[:, :], y_acc[:, :], y_sq[:, n % 2, :], ALU.add).then_inc(*sig("y_acc"))

            def input_squares(l, q):
                pool.wait_ge(*at(l, "h_sum", q + 1))
                pool.tensor_tensor(h_acc[:, :], con[:, 0:NT], con[:, 0:NT], ALU.subtract).then_inc(*sig("h_acc"))
                for k in range(KD):
                    pool.wait_ge(*at(l, "h_sq", 8 * q + k + 1))
                    pool.wait_ge(*at(l, "h_acc", 9 * q + k + 1))
                    pool.tensor_tensor(h_acc[:, :], h_acc[:, :], h_sq[:, k % 2, :], ALU.add).then_inc(*sig("h_acc"))

            def feed_forward(l, q):
                f = q // 2
                def product(j, b, reps):
                    pool.wait_ge(*at(l, "gu_read", f * 44 + 2 * j + 2))
                    pool.wait_ge(*at(l, "silu_ready", f * 22 + j + 1))
                    pool.wait_ge(*at(l, "act_lo", f * 22 + j - 1))
                    pool.tensor_tensor(act_s[:, b, :], silu_s[:, b, :], up_s[:, b, :], ALU.mult).then_inc(*sig("act_ready", reps))

                def rest(j, b, reps):
                    pool.wait_ge(*at(l, "act_hi", f * 22 + j + 1))
                    pool.tensor_tensor(tile_of(act_lo, j), act_s[:, b, :], tile_of(act_hi, j).bitcast(F32), ALU.subtract)\
                        .then_inc(*sig("act_lo", reps))
                product(0, 0, 1)
                with pool.Fori(0, 10) as i:
                    for b in range(2):
                        product(2 * i + b + 1, 1 - b, 10)
                        rest(2 * i + b, b, 10)
                product(21, 1, 1)
                rest(20, 0, 1)
                rest(21, 1, 1)
                output_squares(l, q)
                input_squares(l, q)

            def after(l, **counts):
                for name, k in counts.items():
                    pool.wait_ge(*at(l, name, k))

            def mix(l, n):
                if n == 0:
                    pool.wait_ge(setup, 16 * 3)
                    pool.wait_ge(S["unit_done"], l * UNITS + PHASES["in"][0] + RING)
                    after(l, stored=0)
                    zero = con[:, 0:2 * (TAPS_A - 1)].rearrange("p (a b) -> p a b", a=2)
                    pool.tensor_tensor(a_pad[:, :, 0:TAPS_A - 1], zero, zero, ALU.subtract).then_inc(*sig("a_z"))
                    zero = con[:, 0:H * NT].rearrange("p (a b) -> p a b", a=H)
                    pool.tensor_tensor(qm[:, :, :], zero, zero, ALU.subtract).then_inc(*sig("d_qz"))
                if n == 4:
                    after(l, b_qs=1)
                    pool.tensor_tensor(q_heads[:, :, :], proj[:, BQ, 0:TP].unsqueeze(1).to_broadcast([P, H, TP]),
                                       const("hv", H * DV)[:, ::DV].unsqueeze(2).to_broadcast([P, H, TP]), ALU.mult).then_inc(*sig("b_qb0"))
                    after(l, b_eb=1, b_qb0=1)
                    pool.tensor_tensor(proj[:, BQ, 0:TP], proj[:, BQ, 0:TP], eb[:, 0:TP], ALU.mult).then_inc(*sig("b_qe"))
                if 6 <= n <= 11:
                    i = n - 5
                    after(l, b_E=i)
                    if i >= 2:
                        after(l, b_sc=i)
                    pool.tensor_tensor(q_lv[:, :, :], q_heads[:, :, :], lv[:, 2 + i % 2, :].unsqueeze(1).to_broadcast([P, H, TP]), ALU.mult)\
                        .then_inc(*sig("b_qbl"))
                if n == 10:
                    after(l, a_sg=1, past=PAST)
                    pool.tensor_tensor(a_pad[:, :, TAPS_A - 1:], proj[:, AV:AV + 2, 0:TP], proj[:, AG:AG + 2, 0:TP], ALU.mult).then_inc(*sig("a_in"))
                    pool.tensor_tensor(a_dec[:, :, :, TAPS_A - 1], proj[:, AV:AV + 2, TP:NT], proj[:, AG:AG + 2, TP:NT], ALU.mult)\
                        .then_inc(*sig("a_in"))
                if n == 12:
                    after(l, proj=12, b_eb=1)
                    for j in range(2):
                        pool.tensor_tensor(v_diag[:, j * TD:(j + 1) * TD, :], proj[:, BV + j, TP:NT].unsqueeze(2).to_broadcast([P, TD, DV]),
                                           const("lvm", CH).unsqueeze(1).to_broadcast([P, TD, CH]), ALU.mult).then_inc(*sig("b_vx"))
                    pool.tensor_tensor(st[:, :, :], st[:, :, :], eb[:, TP:NT].unsqueeze(2).to_broadcast([P, TD, DV]), ALU.mult).then_inc(*sig("b_sde"))
                    after(l, b_sg=1)
                    pool.tensor_tensor(sg[:, :, :], sg[:, :, :], proj[:, BG:BG + 2, :], ALU.mult).then_inc(*sig("b_gs"))
                if n == 14:
                    after(l, b_kvd=1, b_sde=1)
                    pool.tensor_tensor(st[:, :, :], st[:, :, :], st_tmp[:, :, :], ALU.add).then_inc(*sig("b_sd"))
                    after(l, a_in=2)
                    for c in range(2):
                        pool.tensor_tensor(a_prod[:, c, :, :], a_dec[:, c, :, :],
                                           par[:, PAR["acw"] + c * TAPS_A:PAR["acw"] + (c + 1) * TAPS_A].unsqueeze(1).to_broadcast([P, TD, TAPS_A]),
                                           ALU.mult).then_inc(*sig("a_dp"))
                if n in (13, 15, 17):
                    first = A_DVE + (n - 13) // 2 * (TAPS_A - A_DVE) // 3
                    for t in range(first, A_DVE + ((n - 13) // 2 + 1) * (TAPS_A - A_DVE) // 3):
                        done = 2 * (t - A_DVE)
                        for c in range(2):
                            x = a_pad[:, c, t:t + TP]
                            w = par[:, PAR["acw"] + c * TAPS_A + t:PAR["acw"] + c * TAPS_A + t + 1].to_broadcast([P, TP])
                            if t == A_DVE:
                                if c == 0:
                                    after(l, a_in=2, h_sum=2)
                                pool.tensor_tensor(a_part[c][:, 0:TP], x, w, ALU.mult).then_inc(*sig("a_ptap"))
                                continue
                            after(l, a_ptap=done - 1 + c)
                            pool.tensor_tensor(a_term[c][:, 0:TP], x, w, ALU.mult).then_inc(*sig("a_pmul"))
                        if t > A_DVE:
                            for c in range(2):
                                after(l, a_pmul=done - 1 + c)
                                pool.tensor_tensor(a_part[c][:, 0:TP], a_part[c][:, 0:TP], a_term[c][:, 0:TP], ALU.add).then_inc(*sig("a_ptap"))
                if n == 16:
                    after(l, d_qm=2, proj=16)
                    for j in range(2):
                        pool.tensor_tensor(pm[:, 2 * j:2 * j + 2, :], qm[:, 2 * j:2 * j + 2, TP:NT],
                                           proj[:, DKK + j, TP:NT].unsqueeze(1).to_broadcast([P, 2, TD]), ALU.mult).then_inc(*sig("d_pm"))
                if n == 24:
                    short_conv(l)

            def short_conv(l):
                after(l, proj=21, b_y=1)
                z, y, zero = z_pad[:, 0, :], ymix[:, YC, :], con[:, 0:2]
                pool.tensor_tensor(z[:, 0:2], zero, zero, ALU.subtract).then_inc(*sig("c_z"))
                pool.tensor_tensor(z[:, 2:], proj[:, CC, 0:TP], proj[:, CX, 0:TP], ALU.mult).then_inc(*sig("c_z"))
                pool.tensor_tensor(z_dec[:, 0, :, 2], proj[:, CC, TP:NT], proj[:, CX, TP:NT], ALU.mult).then_inc(*sig("c_z"))
                after(l, c_z=3)
                done = 0
                for t in range(TAPS_C):
                    out = c_tmp if t else y
                    w = par[:, PAR["ccw"] + t:PAR["ccw"] + t + 1]
                    pool.tensor_tensor(out[:, 0:TP], z[:, t:t + TP], w.to_broadcast([P, TP]), ALU.mult).then_inc(*sig("c_t"))
                    pool.tensor_tensor(out[:, TP:NT], z_dec[:, 0, :, t], w.to_broadcast([P, TD]), ALU.mult).then_inc(*sig("c_t"))
                    done += 2
                    if t:
                        after(l, c_t=done)
                        pool.tensor_tensor(y, y, c_tmp, ALU.add).then_inc(*sig("c_t"))
                        done += 1
                        after(l, c_t=done)
                pool.tensor_tensor(y, y, proj[:, CB, :], ALU.mult).then_inc(*sig("c_y"))

            for n, name in enumerate(("split_done", "unit_done", "gu_read", "y_scaled", "silu_ready", "act_ready", "act_lo", "y_acc", "y_sum", "stored")):
                pool.memset(z_t[:, 0, n:n + 1], 0.0).then_inc(S[name], INIT[name])
            pool.memset(h_acc[:, :], 0.0).then_inc(S["h_acc"], 1)
            for k in range(KD):
                pool.wait_ge(S["h_sq"], k + 1)
                pool.wait_ge(S["h_acc"], k + 1)
                pool.tensor_tensor(h_acc[:, :], h_acc[:, :], h_sq[:, k % 2, :], ALU.add).then_inc(S["h_acc"], 1)
            with pool.Fori(0, L) as l:
                feed_forward(l, 0)
                for n in (0, 4, 6, 7, 8, 9, 10, 11, 12, 13, 14, 15, 16, 17, 24):
                    mix(l, n)
                output_squares(l, 1)
                input_squares(l, 1)
                feed_forward(l, 2)
OUTS = {"h": (P, KD, NT), "kv": (L, P, 4 * NT), "pf": (L, H, TP), "sf": (L, H * TD, 1), "sb": (L, P, TD * DV), "pc": (L, P, 2, 2)}
for _c in range(2):
    OUTS[f"pa{_c}"] = (L, P, TAPS_A - 1)
    OUTS[f"sa{_c}"] = (L, P, TD, TAPS_A - 1)
    OUTS[f"sc{_c}"] = (L, P, TD, 2)
for _h in range(H):
    OUTS[f"pb{_h}"] = (L, DK, DV)


def states_in(a, g):
    import numpy as np
    f = np.ascontiguousarray
    for c in range(2):
        part = slice(c * P, (c + 1) * P)
        a[f"state_a{c}"] = f(g["state_conv_a"][..., part].transpose(0, 3, 1, 2))
        a[f"state_c{c}"] = f(g["state_conv_c"][..., part].transpose(0, 3, 1, 2))
    a["state_b"] = f(g["state_gla"].transpose(0, 2, 3, 1, 4)).reshape(L, P, TD * DV)
    a["cache_k"] = f(g["cache_k"].reshape(L * NPOOL, PAGE, 2, P).transpose(0, 3, 2, 1)).reshape(L * NPOOL, P, 2 * PAGE)
    a["cache_v"] = f(g["cache_v"]).reshape(L * NPOOL, PAGE, H * DV)
    a["cache_f"] = f(g["cache_logf"].transpose(0, 1, 3, 2)).reshape(L * NPOOL, H, PAGE)
    a["table"] = f(g["page_table"]).reshape(1, TD * NPAGES)


def results(r):
    import numpy as np
    h = r["h"].transpose(2, 1, 0).reshape(NT, D)
    kv = r["kv"].reshape(L, P, 2, 2, NT).transpose(2, 0, 4, 3, 1).reshape(2, L, NT, H, DV)
    two = lambda n: np.stack([r[n + "0"], r[n + "1"]], 1)
    pa = two("pa").transpose(0, 3, 1, 2).reshape(L, 1, TAPS_A - 1, 2 * P)
    sa = two("sa").transpose(0, 3, 4, 1, 2).reshape(L, TD, TAPS_A - 1, 2 * P)
    pb = np.stack([r[f"pb{i}"] for i in range(H)], 1).reshape(L, 1, H, DK, DV)
    sb = r["sb"].reshape(L, H, DK, TD, DV).transpose(0, 3, 1, 2, 4)
    pc = r["pc"].transpose(0, 3, 2, 1).reshape(L, 1, 2, 2 * P)
    sc = two("sc").transpose(0, 3, 4, 1, 2).reshape(L, TD, 2, 2 * P)
    pf = r["pf"].transpose(0, 2, 1).reshape(L, 1, TP, H)
    sf = r["sf"].reshape(L, H, TD).transpose(0, 2, 1).reshape(L, TD, 1, H)
    return (h[None, :TP], h[TP:, None], pa, pb, pc, kv[0, :, None, :TP], kv[1, :, None, :TP], pf,
            sa, sb, sc, kv[0, :, TP:, None], kv[1, :, TP:, None], sf)


def build(nc, ins, outs):
    tally = {}
    decoder_kernel(nc, ins, outs, PERS, tally)
    assert tally == PERS, {k: (PERS.get(k), tally.get(k)) for k in set(PERS) | set(tally) if PERS.get(k) != tally.get(k)}


PERS = {
    "past": 336, "keys_in": 256, "stored": 240, "lfn_in": 16, "values_in0": 128, "values_in1": 128, "unit_done":
    168, "h_sum": 3, "y_sum": 3, "b_z": 1, "b_sc": 7, "b_vT": 1, "b_kdT": 1, "b_vb": 1, "b_kv": 1, "d_dsc": 2,
    "b_o": 1, "b_od": 1, "d_new": 1, "d_dT": 1, "d_sc": 4, "d_vT": 1, "b_gn": 1, "d_dpT": 1, "d_dpv": 2,
    "a_sum": 1, "d_pT": 4, "a_var": 1, "d_o": 1, "hi_ready": 168, "rh_ready": 6, "silu_ready": 44, "act_hi": 44,
    "y_sq": 24, "y_scaled": 24, "ry_ready": 6, "hg_hi": 24, "h_sq": 24, "b_qs": 1, "b_sp": 3, "b_eb": 1, "b_E":
    7, "d_sp": 3, "a_sg": 1, "b_sg": 1, "b_vt": 1, "b_kdt": 1, "d_qm": 2, "d_scs": 1, "b_og": 3, "b_osq": 1,
    "d_dex": 1, "d_vt": 1, "d_ptd": 1, "b_rs": 4, "d_ex": 8, "ym_hi": 8, "a_sq": 1, "d_pt": 4, "a_rsd": 2,
    "d_y": 1, "a_y": 2, "split_done": 168, "par_ready": 1, "gu_read": 88, "z_ready": 24, "h_ready": 24,
    "hg_ready": 24, "proj": 24, "b_la": 2, "b_bc": 2, "b_D": 13, "b_kt": 7, "b_msk": 7, "d_lf": 2, "d_cf": 2,
    "b_asc": 6, "a_tap": 40, "b_kvm": 2, "b_S": 3, "b_kvd": 1, "b_prod": 1, "d_ct": 3, "a_dr": 1, "a_db": 1,
    "d_ds": 2, "d_dmx": 1, "d_sm": 4, "d_dri": 1, "d_dp": 2, "d_mx": 2, "a_all": 2, "b_t": 2, "b_y": 1, "d_ri":
    1, "d_pn": 2, "ym_ready": 8, "a_cen": 2, "a_nrm": 1, "c_z1": 3, "c_t1": 6, "c_y1": 1, "d_dt": 1, "d_dy": 2,
    "act_ready": 44, "act_lo": 44, "y_acc": 24, "h_acc": 27, "a_z": 1, "d_qz": 1, "b_qb0": 1, "b_qe": 1,
    "b_qbl": 6, "a_in": 2, "b_vx": 2, "b_sde": 1, "b_gs": 1, "a_ptap": 22, "a_pmul": 20, "b_sd": 1, "a_dp": 2,
    "d_pm": 2, "c_z": 3, "c_t": 8, "c_y": 1
}


def packed(a, k, n):
    import numpy as np
    return np.ascontiguousarray(a.reshape(L, k, P, n, P).transpose(0, 3, 2, 1, 4)).reshape(L * n, P, k * P)


def kernel(**inputs):
    import numpy as np
    import concourse.bacc as _bacc
    from concourse.bass_utils import run_bass_kernel_spmd as _run

    g = {k: np.asarray(v) for k, v in inputs.items()}
    f32 = np.float32
    a = {}

    for f in (0, 1):
        gate, up = (packed(g[f"ffn{f + 1}_w_{n}"], KD, KF) for n in ("gate", "up"))
        gu = np.stack([gate, up], 1).reshape(L * 44, P, COLS)
        a[f"w_gu{f}"] = np.concatenate([gu, np.zeros((LEAD, P, COLS), f32)])
        dn = packed(g[f"ffn{f + 1}_w_down"], KF, KD)
        dn = np.concatenate([dn, np.zeros((L * KD, P, 2 * P), f32)], 2)
        a[f"w_dn{f}"] = np.ascontiguousarray(dn.reshape(L * KD, P, 3, COLS).transpose(0, 2, 1, 3)).reshape(L * 24, P, COLS)
    order = {YA: 0, YB: 2, YC: 4, YD: 6}
    rows = [order[t - t % 2] + t % 2 for t in range(KD)]
    a["w_out"] = packed(g["w_out"].reshape(L, KD, P, D)[:, rows].reshape(L, D, D), KD, KD)
    w = g["w_in"]
    off_b, off_c, off_d = 512, 512 + 784, 512 + 784 + 768
    at = {ALR: off_b + 768, FG: off_d + 768, BQ: off_b, BK: off_b + 128, AV: 0, AV + 1: 128, AG: 256, AG + 1: 384,
          BG: off_b + 512, BG + 1: off_b + 640, BV: off_b + 256, BV + 1: off_b + 384}
    for i in range(6):
        at[DQ + i] = off_d + i * P
        at[CB + i] = off_c + (i % 3 * 2 + i // 3) * P
    win = np.zeros((L, 24, P, COLS), f32)
    for n in range(24):
        m = IN_WIDTH[n]
        win[:, n, :, 0:KD * m] = w[:, :, at[n]:at[n] + m].reshape(L, KD, P, m).transpose(0, 2, 1, 3).reshape(L, P, KD * m)
    a["w_in"] = win.reshape(L * 24, P, COLS)

    def tiles(x):
        return x.reshape(L, -1, P).transpose(2, 0, 1)

    par = np.zeros((P, L, NPAR), f32)

    def put(name, x, off=0):
        par[0:x.shape[0], :, PAR[name] + off:PAR[name] + off + x.shape[2]] = x
    put("pre", tiles(g["mix_pre_g"]), 0)
    put("pre", tiles(g["ffn2_pre_g"]), 8)
    put("pre", np.roll(tiles(g["ffn1_pre_g"]), -1, 1), 16)
    put("post", tiles(g["ffn1_post_g"]), 0)
    put("post", tiles(g["mix_post_g"]), 8)
    put("post", tiles(g["ffn2_post_g"]), 16)
    put("acw", g["a_conv_w"].reshape(L, TAPS_A, 2, P).transpose(3, 0, 2, 1).reshape(P, L, 62))
    put("acb", tiles(g["a_conv_b"]))
    put("alg", tiles(g["a_ln_g"]))
    put("alb", tiles(g["a_ln_b"]))
    put("ba", tiles(g["b_gate_b"]))
    put("bng", tiles(g["b_out_norm_g"]))
    put("ccw", g["c_conv_w"].reshape(L, TAPS_C, 2, P).transpose(3, 0, 2, 1).reshape(P, L, 6))
    put("bf", g["d_forget_b"].T.reshape(H, L, 1))
    put("wa2", g["b_gate_w2"].transpose(1, 0, 2))
    a["par"] = par
    a["gain0"] = np.ascontiguousarray(tiles(g["ffn1_pre_g"])[:, 0])

    con = np.zeros((P, NCON), f32)

    def const(name, x):
        con[0:x.shape[0], CON[name]:CON[name] + x.shape[1]] = x
    p = np.arange(P)
    const("ident", np.eye(P, dtype=f32))
    const("ones", np.ones((P, TP), f32))
    const("blk", (p[:, None] // DV == p[None, :] // DV).astype(f32))
    tri = np.where(p[None, :] <= p[:, None], 0.0, -1e30).astype(f32)
    const("tri", np.concatenate([tri, np.zeros((P, P), f32), tri], 1))
    s, t = p[:, None] % CH, np.arange(CH)[None, :]
    masks = [(s == t) if m == 0 else (s // (2 * m) == t // (2 * m)) & (s % (2 * m) < m) & (t % (2 * m) >= m) for m in LEVELS]
    const("lvm", np.concatenate(masks, 1).astype(f32))
    const("rst", np.broadcast_to((np.arange(TP) % CH != 0).astype(f32), (P, TP)))
    const("hv", (p[:, None] // DK == np.arange(H * DV)[None, :] // DV).astype(f32))
    const("sel", (np.arange(H)[:, None] == np.arange(H * P)[None, :] // P).astype(f32))
    const("hvt", np.concatenate([2 * j + p[:, None] // DV == p[None, :] // DK for j in range(2)], 1).astype(f32))
    r = np.arange(H * TD)[:, None]
    const("heads", (r // TD == np.arange(2 * P)[None, :] // DV).astype(f32))
    const("dec", (r % TD == np.arange(TD)[None, :]).astype(f32))
    a["con"] = con

    x = np.concatenate([g["x_prompt"].reshape(TP, D), g["x_sample"].reshape(TD, D)])
    a["x"] = np.ascontiguousarray(x.T.reshape(KD, P, NT).transpose(1, 0, 2))
    states_in(a, g)

    nc = _bacc.Bacc("TRN2", target_bir_lowering=False, num_devices=1)
    ins = {n: nc.dram_tensor("in_" + n, v.shape, mybir.dt.from_np(v.dtype), kind="ExternalInput").ap() for n, v in a.items()}
    outs = {n: nc.dram_tensor("out_" + n, s, F32, kind="ExternalOutput").ap() for n, s in OUTS.items()}
    build(nc, ins, outs)
    r = _run(nc, [{"in_" + n: v for n, v in a.items()}], core_ids=[0]).results[0]
    return results({n: np.asarray(r["out_" + n]) for n in OUTS})
```
